# Optimizing a Trainium2 kernel written in Bass

```python
import math
import jax, jax.numpy as jnp
from jax import lax
import numpy as np

D_MODEL = 1024
BATCH = 1
SEQ = 512
DEPTH = 1

ATTN_GROUPS = ((128, 1), (512, 4), (2048, 16))
N_ATTN_GROUPS = len(ATTN_GROUPS)
HEADS_PER_GROUP = 6
ATTN_HEADS = N_ATTN_GROUPS * HEADS_PER_GROUP
HEAD_DIM = 64
ATTN_WIDTH = ATTN_HEADS * HEAD_DIM
ATTN_OUT_WIDTH = HEADS_PER_GROUP * HEAD_DIM
REL_BUCKETS = 32
REL_MAX_DISTANCE = 2048
POOL_WINDOWS = (2, 4, 8, 16)
POOL_WIDTH = D_MODEL
POOL_GROUP = POOL_WIDTH // len(POOL_WINDOWS)
SSD_INNER = D_MODEL
SSD_HEAD_DIM = 64
SSD_HEADS = SSD_INNER // SSD_HEAD_DIM
SSD_GROUPS = 2
SSD_STATE = 128
SSD_CONV = 4
SSD_CHUNK = 128
SSD_XBC = SSD_INNER + 2 * SSD_GROUPS * SSD_STATE
D_FF = 2816
FFN_CONV = 3
N_BRANCH = 3
NORM_EPS = 1e-6
IN_SPLIT_SIZES = (ATTN_WIDTH, ATTN_WIDTH, ATTN_WIDTH, POOL_WIDTH, SSD_INNER, SSD_XBC, SSD_HEADS, N_BRANCH * D_MODEL)
IN_WIDTH = sum(IN_SPLIT_SIZES)


def rmsnorm(x, g):
    xf = x.astype(jnp.float32)
    y = xf * lax.rsqrt(jnp.mean(xf * xf, axis=-1, keepdims=True) + NORM_EPS)
    return (y * g.astype(jnp.float32)).astype(x.dtype)

def causal_dwconv(x, w, b):
    K = w.shape[0]
    s = x.shape[1]
    xp = jnp.pad(x, ((0, 0), (K - 1, 0), (0, 0)))
    y = xp[:, 0:s] * w[0]
    for k in range(1, K):
        y = y + xp[:, k:k + s] * w[k]
    return y + b

def t5_bucket(dist):
    max_exact = REL_BUCKETS // 2
    is_small = dist < max_exact
    nf = jnp.maximum(dist, 1).astype(jnp.float32)
    large = max_exact + (jnp.log(nf / max_exact) / math.log(REL_MAX_DISTANCE / max_exact)
                         * (REL_BUCKETS - max_exact)).astype(jnp.int32)
    large = jnp.minimum(large, REL_BUCKETS - 1)
    return jnp.where(is_small, dist, large)

def dilated_group_attention(q, k, v, bias_table, dilation, steps):
    b, s, h, dh = q.shape
    L = s // dilation
    W = steps
    nb = -(-L // W)
    Lp = nb * W
    bd = b * dilation

    def to_res(t):
        return t.reshape(b, L, dilation, h, dh).transpose(0, 2, 3, 1, 4).reshape(bd, h, L, dh)

    qb = jnp.pad(to_res(q), ((0, 0), (0, 0), (0, Lp - L), (0, 0))).reshape(bd, h, nb, W, dh)
    kr = jnp.pad(to_res(k), ((0, 0), (0, 0), (W, Lp - L), (0, 0))).reshape(bd, h, nb + 1, W, dh)
    vr = jnp.pad(to_res(v), ((0, 0), (0, 0), (W, Lp - L), (0, 0))).reshape(bd, h, nb + 1, W, dh)
    kb = jnp.concatenate([kr[:, :, :-1], kr[:, :, 1:]], axis=3)
    vb = jnp.concatenate([vr[:, :, :-1], vr[:, :, 1:]], axis=3)

    qi = jnp.arange(W)[:, None]
    kk = jnp.arange(2 * W)[None, :]
    rel = qi + W - kk
    band = (rel >= 0) & (rel <= W)
    kabs = jnp.arange(nb)[:, None, None] * W + kk[None] - W
    valid = band[None] & (kabs >= 0)
    bucket = t5_bucket(jnp.clip(rel, 0, None) * dilation)
    bias = bias_table[bucket].transpose(2, 0, 1).astype(jnp.float32)

    scale = 1.0 / math.sqrt(dh)
    scores = jnp.einsum("bhnqd,bhnkd->bhnqk", qb, kb).astype(jnp.float32) * scale + bias[:, None]
    scores = jnp.where(valid[None, None], scores, -jnp.inf)
    m = jnp.max(scores, axis=-1, keepdims=True)
    p = jnp.exp(scores - m)
    l = jnp.sum(p, axis=-1)
    o = jnp.einsum("bhnqk,bhnkd->bhnqd", p, vb.astype(jnp.float32)) / l[..., None]
    lse = m[..., 0] + jnp.log(l)

    o = o.reshape(bd, h, Lp, dh)[:, :, :L].reshape(b, dilation, h, L, dh)
    o = o.transpose(0, 3, 1, 2, 4).reshape(b, s, h, dh)
    lse = lse.reshape(bd, h, Lp)[:, :, :L].reshape(b, dilation, h, L)
    lse = lse.transpose(0, 3, 1, 2).reshape(b, s, h)
    return o, lse

def dilated_attention_mixer(q, k, v, rel_bias):
    b, s = q.shape[:2]
    outs, lses = [], []
    for gi, (window, dilation) in enumerate(ATTN_GROUPS):
        hs = slice(gi * HEADS_PER_GROUP, (gi + 1) * HEADS_PER_GROUP)
        o, lse = dilated_group_attention(q[:, :, hs], k[:, :, hs], v[:, :, hs],
                                         rel_bias[:, hs], dilation, window // dilation)
        outs.append(o)
        lses.append(lse)
    o = jnp.stack(outs, axis=0)
    alpha = jax.nn.softmax(jnp.stack(lses, axis=0), axis=0)
    o = jnp.sum(alpha[..., None] * o, axis=0)
    return o.reshape(b, s, ATTN_OUT_WIDTH).astype(q.dtype)

def pool_mixer(u, w_grp, scale):
    b, s, _ = u.shape
    uf = u.astype(jnp.float32)
    cs = jnp.cumsum(uf, axis=1)
    pos = (jnp.arange(s) + 1)[None, :, None]
    outs = []
    for gi, w in enumerate(POOL_WINDOWS):
        sl = slice(gi * POOL_GROUP, (gi + 1) * POOL_GROUP)
        c = cs[..., sl]
        shifted = jnp.pad(c, ((0, 0), (w, 0), (0, 0)))[:, :s]
        cnt = jnp.minimum(pos, w).astype(jnp.float32)
        outs.append((c - shifted) / cnt - uf[..., sl])
    d = jnp.stack(outs, axis=2).astype(u.dtype)
    y = jnp.einsum("bsgc,gcd->bsgd", d, w_grp).reshape(b, s, POOL_WIDTH)
    return y * scale

def ssd_scan(x, dt, A, Bm, Cm):
    b, s, h, p = x.shape
    g, n = Bm.shape[2:]
    e = h // g
    l = SSD_CHUNK
    c = s // l
    xc = (x * dt[..., None]).reshape(b, c, l, g, e, p)
    a = (dt * A).reshape(b, c, l, h).transpose(0, 3, 1, 2)
    a_cs = jnp.cumsum(a, axis=-1)
    Bc = Bm.reshape(b, c, l, g, n)
    Cc = Cm.reshape(b, c, l, g, n)
    causal = jnp.tril(jnp.ones((l, l), dtype=bool))
    seg = a_cs[..., :, None] - a_cs[..., None, :]
    Lmat = jnp.exp(jnp.where(causal, seg, -jnp.inf)).reshape(b, g, e, c, l, l)
    cb = jnp.einsum("bclgn,bcsgn->bcgls", Cc, Bc)
    y_diag = jnp.einsum("bcgls,bgecls,bcsgep->bclgep", cb, Lmat, xc)
    decay = jnp.exp(a_cs[..., -1:] - a_cs).reshape(b, g, e, c, l)
    states = jnp.einsum("bclgn,bgecl,bclgep->bcgepn", Bc, decay, xc)
    chunk_decay = jnp.exp(a_cs[..., -1]).reshape(b, g, e, c)

    def step(carry, inp):
        st, dec = inp
        return carry * dec[..., None, None] + st, carry

    init = jnp.zeros((b, g, e, p, n), dtype=x.dtype)
    _, prev = lax.scan(step, init, (states.transpose(1, 0, 2, 3, 4, 5), chunk_decay.transpose(3, 0, 1, 2)))
    prev = prev.transpose(1, 0, 2, 3, 4, 5)
    out_decay = jnp.exp(a_cs).reshape(b, g, e, c, l)
    y_off = jnp.einsum("bclgn,bcgepn,bgecl->bclgep", Cc, prev, out_decay)
    return (y_diag + y_off).reshape(b, s, h, p)

def ssd_mixer(z, xbc, dt_raw, conv_w, conv_b, dt_bias, a_log, d_skip, norm_w):
    b, s, _ = z.shape
    xbc = jax.nn.silu(causal_dwconv(xbc, conv_w, conv_b))
    xs = xbc[..., :SSD_INNER].reshape(b, s, SSD_HEADS, SSD_HEAD_DIM).astype(jnp.float32)
    Bm = xbc[..., SSD_INNER:SSD_INNER + SSD_GROUPS * SSD_STATE].reshape(b, s, SSD_GROUPS, SSD_STATE).astype(jnp.float32)
    Cm = xbc[..., SSD_INNER + SSD_GROUPS * SSD_STATE:].reshape(b, s, SSD_GROUPS, SSD_STATE).astype(jnp.float32)
    dt = jax.nn.softplus(dt_raw.astype(jnp.float32) + dt_bias.astype(jnp.float32))
    A = -jnp.exp(a_log.astype(jnp.float32))
    y = ssd_scan(xs, dt, A, Bm, Cm) + d_skip.astype(jnp.float32)[:, None] * xs
    y = y.reshape(b, s, SSD_INNER) * jax.nn.silu(z.astype(jnp.float32))
    yg = y.reshape(b, s, SSD_GROUPS, SSD_INNER // SSD_GROUPS)
    yg = yg * lax.rsqrt(jnp.mean(yg * yg, axis=-1, keepdims=True) + NORM_EPS)
    y = yg.reshape(b, s, SSD_INNER) * norm_w.astype(jnp.float32)
    return y.astype(z.dtype)

def conv_ffn(u, w_up, conv_w, conv_b, w_down):
    h = causal_dwconv(u @ w_up, conv_w, conv_b)
    a, v = h[..., :D_FF], h[..., D_FF:]
    return (jax.nn.silu(a) * v) @ w_down

def first_inputs(seed: int = 0) -> dict:
    key = jax.random.key(seed)
    ks = jax.random.split(key, 24)
    f32 = jnp.float32

    def nrm(k, shape, scale):
        return jax.random.normal(k, shape, dtype=f32) * scale

    dt0 = jnp.exp(jax.random.uniform(ks[10], (DEPTH, SSD_HEADS), dtype=f32)
                  * (math.log(0.1) - math.log(0.001)) + math.log(0.001))
    return {
        "x": nrm(ks[0], (BATCH, SEQ, D_MODEL), 1.0),
        "rel_bias": nrm(ks[1], (REL_BUCKETS, ATTN_HEADS), 0.1),
        "ln1_g": 1.0 + nrm(ks[2], (DEPTH, D_MODEL), 0.02),
        "w_in": nrm(ks[3], (DEPTH, D_MODEL, IN_WIDTH), D_MODEL ** -0.5),
        "b_gate": nrm(ks[4], (DEPTH, N_BRANCH * D_MODEL), 0.02),
        "w_a": nrm(ks[5], (DEPTH, ATTN_OUT_WIDTH, D_MODEL), ATTN_OUT_WIDTH ** -0.5),
        "pool_w": nrm(ks[6], (DEPTH, len(POOL_WINDOWS), POOL_GROUP, POOL_GROUP), POOL_GROUP ** -0.5),
        "pool_scale": 1.0 + nrm(ks[7], (DEPTH, POOL_WIDTH), 0.1),
        "w_b": nrm(ks[8], (DEPTH, POOL_WIDTH, D_MODEL), POOL_WIDTH ** -0.5),
        "ssd_conv_w": nrm(ks[9], (DEPTH, SSD_CONV, SSD_XBC), SSD_CONV ** -0.5),
        "ssd_conv_b": nrm(ks[11], (DEPTH, SSD_XBC), 0.02),
        "ssd_dt_bias": dt0 + jnp.log(-jnp.expm1(-dt0)),
        "ssd_a_log": jnp.log(jax.random.uniform(ks[12], (DEPTH, SSD_HEADS), dtype=f32, minval=1.0, maxval=16.0)),
        "ssd_d": 1.0 + nrm(ks[13], (DEPTH, SSD_HEADS), 0.1),
        "ssd_norm_w": 1.0 + nrm(ks[14], (DEPTH, SSD_INNER), 0.02),
        "w_c": nrm(ks[15], (DEPTH, SSD_INNER, D_MODEL), SSD_INNER ** -0.5),
        "w_o": nrm(ks[16], (DEPTH, D_MODEL, D_MODEL), D_MODEL ** -0.5),
        "ln2_g": 1.0 + nrm(ks[17], (DEPTH, D_MODEL), 0.02),
        "ffn_w_up": nrm(ks[18], (DEPTH, D_MODEL, 2 * D_FF), D_MODEL ** -0.5),
        "ffn_conv_w": nrm(ks[19], (DEPTH, FFN_CONV, 2 * D_FF), FFN_CONV ** -0.5),
        "ffn_conv_b": nrm(ks[20], (DEPTH, 2 * D_FF), 0.02),
        "ffn_w_down": nrm(ks[21], (DEPTH, D_FF, D_MODEL), D_FF ** -0.5),
        "final_g": 1.0 + nrm(ks[22], (D_MODEL,), 0.02),
    }

def first_block(x, rel_bias, ln1_g, w_in, b_gate, w_a, pool_w, pool_scale, w_b,
              ssd_conv_w, ssd_conv_b, ssd_dt_bias, ssd_a_log, ssd_d, ssd_norm_w, w_c,
              w_o, ln2_g, ffn_w_up, ffn_conv_w, ffn_conv_b, ffn_w_down, final_g):
    b, s, _ = x.shape
    split_idx = []
    acc = 0
    for sz in IN_SPLIT_SIZES[:-1]:
        acc += sz
        split_idx.append(acc)
    for i in range(DEPTH):
        u = rmsnorm(x, ln1_g[i])
        proj = u @ w_in[i]
        q, k, v, pool_in, z, xbc, dt_raw, gate_pre = jnp.split(proj, split_idx, axis=-1)
        q = q.reshape(b, s, ATTN_HEADS, HEAD_DIM)
        k = k.reshape(b, s, ATTN_HEADS, HEAD_DIM)
        v = v.reshape(b, s, ATTN_HEADS, HEAD_DIM)
        y_a = dilated_attention_mixer(q, k, v, rel_bias) @ w_a[i]
        y_b = pool_mixer(pool_in, pool_w[i], pool_scale[i]) @ w_b[i]
        y_c = ssd_mixer(z, xbc, dt_raw, ssd_conv_w[i], ssd_conv_b[i], ssd_dt_bias[i],
                        ssd_a_log[i], ssd_d[i], ssd_norm_w[i]) @ w_c[i]
        gates = jax.nn.sigmoid(gate_pre + b_gate[i]).reshape(b, s, N_BRANCH, D_MODEL)
        merged = gates[:, :, 0] * y_a + gates[:, :, 1] * y_b + gates[:, :, 2] * y_c
        x = x + merged @ w_o[i]
        x = x + conv_ffn(rmsnorm(x, ln2_g[i]), ffn_w_up[i], ffn_conv_w[i], ffn_conv_b[i], ffn_w_down[i])
    return rmsnorm(x, final_g)


DEPTH_2 = 2

GRID_W = 64
Q_BLOCK = 128
RET_CHUNK = 128

DIFF_HEADS = 4
DIFF_HEAD_DIM = 64
DIFF_V_DIM = 2 * DIFF_HEAD_DIM
DIFF_WIDTH = DIFF_HEADS * DIFF_V_DIM
PARTIAL_ROT_DIM = DIFF_HEAD_DIM // 4
PARTIAL_ROPE_THETA = 500000.0

RET_HEADS = 4
RET_KEY_DIM = 128
RET_VAL_DIM = 128
RET_WIDTH = RET_HEADS * RET_VAL_DIM
RET_ROPE_THETA = 10000.0

GQA_Q_HEADS = 8
GQA_KV_HEADS = 2
GQA_GROUP = GQA_Q_HEADS // GQA_KV_HEADS
GQA_HEAD_DIM = 64
GQA_WIDTH = GQA_Q_HEADS * GQA_HEAD_DIM
AXIAL_DIM = GQA_HEAD_DIM // 2
AXIAL_ROPE_THETA = 10000.0

N_BRANCHES = 3
BRANCH_WIDTH = 512
D_FF_2 = 4 * D_MODEL

IN_SPLITS = (
    DIFF_HEADS * 2 * DIFF_HEAD_DIM,
    DIFF_HEADS * 2 * DIFF_HEAD_DIM,
    DIFF_WIDTH,
    RET_HEADS * RET_KEY_DIM,
    RET_HEADS * RET_KEY_DIM,
    RET_WIDTH,
    RET_WIDTH,
    GQA_Q_HEADS * GQA_HEAD_DIM,
    GQA_KV_HEADS * GQA_HEAD_DIM,
    GQA_KV_HEADS * GQA_HEAD_DIM,
    N_BRANCHES * D_MODEL,
)
IN_COLS = 7424


def rms_norm(x, gain, eps=NORM_EPS):
    xf = x.astype(jnp.float32)
    y = xf * lax.rsqrt(jnp.mean(xf * xf, axis=-1, keepdims=True) + eps)
    return (y * gain.astype(jnp.float32)).astype(x.dtype)

def rope_cos_sin(pos, dim, theta):
    inv_freq = theta ** (-jnp.arange(0, dim, 2, dtype=jnp.float32) / dim)
    ang = pos[:, None] * inv_freq[None, :]
    return jnp.cos(ang), jnp.sin(ang)

def apply_rope(x, cos_sin):
    cos, sin = cos_sin
    n = x.shape[-1] // 2
    shape = (1, cos.shape[0]) + (1,) * (x.ndim - 3) + (n,)
    c = cos.reshape(shape).astype(x.dtype)
    s = sin.reshape(shape).astype(x.dtype)
    x1, x2 = x[..., :n], x[..., n:]
    return jnp.concatenate([x1 * c - x2 * s, x2 * c + x1 * s], axis=-1)

def split_cols(y, sizes):
    out, start = [], 0
    for n in sizes:
        out.append(y[..., start:start + n])
        start += n
    return out

def sweep_query_blocks(fn, q):
    B, S = q.shape[:2]
    nb = S // Q_BLOCK
    qb = jnp.moveaxis(q.reshape((B, nb, Q_BLOCK) + q.shape[2:]), 1, 0)
    ob = lax.map(fn, qb)
    return jnp.moveaxis(ob, 0, 1).reshape((B, S) + ob.shape[3:])

def differential_attention(q, k, v, lam):
    scale = DIFF_HEAD_DIM ** -0.5

    def block(qb):
        s = jnp.einsum('bqhmd,bkhmd->bhmqk', qb, k).astype(jnp.float32) * scale
        p = jax.nn.softmax(s, axis=-1)
        w = (p[:, :, 0] - lam * p[:, :, 1]).astype(v.dtype)
        return jnp.einsum('bhqk,bkhe->bqhe', w, v)

    return sweep_query_blocks(block, q)

def grouped_query_attention(q, k, v):
    scale = GQA_HEAD_DIM ** -0.5

    def block(qb):
        s = jnp.einsum('bqgrd,bkgd->bgrqk', qb, k).astype(jnp.float32) * scale
        p = jax.nn.softmax(s, axis=-1).astype(v.dtype)
        return jnp.einsum('bgrqk,bkgd->bqgrd', p, v)

    return sweep_query_blocks(block, q)

def bidirectional_retention(q, k, v, log_fwd, log_bwd):
    B, S, H, dk = q.shape
    dv = v.shape[-1]
    C = RET_CHUNK
    N = S // C
    q = q.reshape(B, N, C, H, dk)
    k = k.reshape(B, N, C, H, dk)
    v = v.reshape(B, N, C, H, dv)
    i = jnp.arange(C, dtype=jnp.float32)
    diff = i[:, None] - i[None, :]
    decay_intra = jnp.where(
        diff[None] >= 0,
        jnp.exp(jnp.maximum(diff, 0.0)[None] * log_fwd[:, None, None]),
        jnp.exp(jnp.maximum(-diff, 0.0)[None] * log_bwd[:, None, None]))
    scores = jnp.einsum('bnihd,bnjhd->bnhij', q, k) * decay_intra
    out = jnp.einsum('bnhij,bnjhe->bnihe', scores, v)

    zeta_f = jnp.exp((C - 1 - i)[None] * log_fwd[:, None])
    xi_f = jnp.exp((i + 1)[None] * log_fwd[:, None])
    zeta_b = jnp.exp(i[None] * log_bwd[:, None])
    xi_b = jnp.exp((C - i)[None] * log_bwd[:, None])
    kv_f = jnp.einsum('bnjhd,bnjhe,hj->nbhde', k, v, zeta_f)
    kv_b = jnp.einsum('bnjhd,bnjhe,hj->nbhde', k, v, zeta_b)
    dec_f = jnp.exp(C * log_fwd)[None, :, None, None]
    dec_b = jnp.exp(C * log_bwd)[None, :, None, None]

    def chunk_states(kv, decay, reverse):
        def step(state, kv_n):
            return state * decay + kv_n, state
        _, states = lax.scan(step, jnp.zeros_like(kv[0]), kv, reverse=reverse)
        return states

    s_f = chunk_states(kv_f, dec_f, False)
    s_b = chunk_states(kv_b, dec_b, True)
    out = (out
           + jnp.einsum('bnihd,nbhde,hi->bnihe', q, s_f, xi_f)
           + jnp.einsum('bnihd,nbhde,hi->bnihe', q, s_b, xi_b))
    return out.reshape(B, S, H, dv)

def head_group_norm(x, gain, eps=1e-5):
    xf = x.astype(jnp.float32)
    mu = jnp.mean(xf, axis=-1, keepdims=True)
    var = jnp.mean(jnp.square(xf - mu), axis=-1, keepdims=True)
    y = ((xf - mu) * lax.rsqrt(var + eps)).reshape(x.shape[0], x.shape[1], -1)
    return y * gain.astype(jnp.float32)

def second_inputs(seed: int = 0) -> dict:
    key = jax.random.key(seed)
    ks = jax.random.split(key, 21)
    L, D = DEPTH_2, D_MODEL
    f32 = jnp.float32

    def normal(k, shape, scale):
        return jax.random.normal(k, shape, f32) * scale

    def gain(k, shape):
        return 1.0 + 0.02 * jax.random.normal(k, shape, f32)

    base_log_decay = jnp.log(-jnp.log1p(-(2.0 ** (-5.0 - jnp.arange(RET_HEADS, dtype=f32)))))
    return {
        "x": jax.random.normal(ks[0], (BATCH, SEQ, D), f32),
        "attn_norm": gain(ks[1], (L, D)),
        "w_in": normal(ks[2], (L, D, IN_COLS), D ** -0.5),
        "diff_q_norm": gain(ks[3], (L, DIFF_HEAD_DIM)),
        "diff_k_norm": gain(ks[4], (L, DIFF_HEAD_DIM)),
        "diff_lam_q1": normal(ks[5], (L, DIFF_HEAD_DIM), 0.1),
        "diff_lam_k1": normal(ks[6], (L, DIFF_HEAD_DIM), 0.1),
        "diff_lam_q2": normal(ks[7], (L, DIFF_HEAD_DIM), 0.1),
        "diff_lam_k2": normal(ks[8], (L, DIFF_HEAD_DIM), 0.1),
        "diff_subln": gain(ks[9], (L, DIFF_V_DIM)),
        "ret_decay_fwd": base_log_decay[None] + normal(ks[10], (L, RET_HEADS), 0.1),
        "ret_decay_bwd": base_log_decay[None] + normal(ks[11], (L, RET_HEADS), 0.1),
        "ret_group_norm": gain(ks[12], (L, RET_WIDTH)),
        "gqa_q_norm": gain(ks[13], (L, GQA_HEAD_DIM)),
        "gqa_k_norm": gain(ks[14], (L, GQA_HEAD_DIM)),
        "w_branch": normal(ks[15], (L, N_BRANCHES, BRANCH_WIDTH, D), BRANCH_WIDTH ** -0.5),
        "w_out": normal(ks[16], (L, D, D), D ** -0.5),
        "mlp_norm": gain(ks[17], (L, D)),
        "w_mlp_in": normal(ks[18], (L, D, D_FF_2), D ** -0.5),
        "w_mlp_out": normal(ks[19], (L, D_FF_2, D), D_FF_2 ** -0.5),
    }

def second_block(x, attn_norm, w_in, diff_q_norm, diff_k_norm, diff_lam_q1, diff_lam_k1,
              diff_lam_q2, diff_lam_k2, diff_subln, ret_decay_fwd, ret_decay_bwd,
              ret_group_norm, gqa_q_norm, gqa_k_norm, w_branch, w_out, mlp_norm,
              w_mlp_in, w_mlp_out):
    B, S, D = x.shape
    f32 = jnp.float32
    rows = S // GRID_W
    seq_pos = jnp.arange(S, dtype=f32)
    row_pos = jnp.repeat(jnp.arange(rows, dtype=f32), GRID_W)
    col_pos = jnp.tile(jnp.arange(GRID_W, dtype=f32), rows)
    rope_partial = rope_cos_sin(seq_pos, PARTIAL_ROT_DIM, PARTIAL_ROPE_THETA)
    rope_ret = rope_cos_sin(seq_pos, RET_KEY_DIM, RET_ROPE_THETA)
    rope_row = rope_cos_sin(row_pos, AXIAL_DIM, AXIAL_ROPE_THETA)
    rope_col = rope_cos_sin(col_pos, AXIAL_DIM, AXIAL_ROPE_THETA)

    def partial_rope(t):
        return jnp.concatenate([apply_rope(t[..., :PARTIAL_ROT_DIM], rope_partial),
                                t[..., PARTIAL_ROT_DIM:]], axis=-1)

    def axial_rope(t):
        return jnp.concatenate([apply_rope(t[..., :AXIAL_DIM], rope_row),
                                apply_rope(t[..., AXIAL_DIM:], rope_col)], axis=-1)

    h = x
    for l in range(DEPTH_2):
        u = rms_norm(h, attn_norm[l])
        proj = jnp.einsum('bsd,dc->bsc', u, w_in[l])
        (dq, dk, dv, rq, rk, rv, rg, gq, gk, gv, gate_logits) = split_cols(proj, IN_SPLITS)

        lambda_init = 0.8 - 0.6 * math.exp(-0.3 * l)
        lam = (jnp.exp(jnp.sum(diff_lam_q1[l].astype(f32) * diff_lam_k1[l].astype(f32)))
               - jnp.exp(jnp.sum(diff_lam_q2[l].astype(f32) * diff_lam_k2[l].astype(f32)))
               + lambda_init)
        dq = partial_rope(rms_norm(dq.reshape(B, S, DIFF_HEADS, 2, DIFF_HEAD_DIM), diff_q_norm[l]))
        dk = partial_rope(rms_norm(dk.reshape(B, S, DIFF_HEADS, 2, DIFF_HEAD_DIM), diff_k_norm[l]))
        dv = dv.reshape(B, S, DIFF_HEADS, DIFF_V_DIM)
        a = differential_attention(dq, dk, dv, lam)
        a = (rms_norm(a, diff_subln[l], eps=1e-5) * (1.0 - lambda_init)).reshape(B, S, DIFF_WIDTH)

        rq = apply_rope(rq.reshape(B, S, RET_HEADS, RET_KEY_DIM), rope_ret).astype(f32)
        rk = (apply_rope(rk.reshape(B, S, RET_HEADS, RET_KEY_DIM), rope_ret).astype(f32)
              * (RET_KEY_DIM ** -0.5))
        rv = rv.reshape(B, S, RET_HEADS, RET_VAL_DIM).astype(f32)
        log_fwd = -jnp.exp(ret_decay_fwd[l].astype(f32))
        log_bwd = -jnp.exp(ret_decay_bwd[l].astype(f32))
        r = bidirectional_retention(rq, rk, rv, log_fwd, log_bwd)
        r = (jax.nn.silu(rg.astype(f32)) * head_group_norm(r, ret_group_norm[l])).astype(h.dtype)

        gq = axial_rope(rms_norm(gq.reshape(B, S, GQA_KV_HEADS, GQA_GROUP, GQA_HEAD_DIM), gqa_q_norm[l]))
        gk = axial_rope(rms_norm(gk.reshape(B, S, GQA_KV_HEADS, GQA_HEAD_DIM), gqa_k_norm[l]))
        gv = gv.reshape(B, S, GQA_KV_HEADS, GQA_HEAD_DIM)
        c = grouped_query_attention(gq, gk, gv).reshape(B, S, GQA_WIDTH)

        branches = jnp.stack([a, r, c], axis=2)
        projected = jnp.einsum('bsnw,nwd->bsnd', branches, w_branch[l])
        gates = jax.nn.sigmoid(gate_logits.reshape(B, S, N_BRANCHES, D))
        merged = jnp.sum(gates * projected, axis=2)
        h = h + jnp.einsum('bsd,de->bse', merged, w_out[l])

        m = jnp.einsum('bsd,df->bsf', rms_norm(h, mlp_norm[l]), w_mlp_in[l])
        m = jnp.square(jax.nn.relu(m))
        h = h + jnp.einsum('bsf,fd->bsd', m, w_mlp_out[l])
    return h


def setup_inputs(seed=0):
    out = dict(first_inputs(seed))
    for name, value in second_inputs(seed + 1).items():
        if name != "x":
            out[name + "_2"] = value
    return out


def reference(
    x, rel_bias, ln1_g, w_in, b_gate, w_a, pool_w, pool_scale, w_b, ssd_conv_w, ssd_conv_b,
    ssd_dt_bias, ssd_a_log, ssd_d, ssd_norm_w, w_c, w_o, ln2_g, ffn_w_up, ffn_conv_w,
    ffn_conv_b, ffn_w_down, final_g, attn_norm_2, w_in_2, diff_q_norm_2, diff_k_norm_2,
    diff_lam_q1_2, diff_lam_k1_2, diff_lam_q2_2, diff_lam_k2_2, diff_subln_2, ret_decay_fwd_2,
    ret_decay_bwd_2, ret_group_norm_2, gqa_q_norm_2, gqa_k_norm_2, w_branch_2, w_out_2,
    mlp_norm_2, w_mlp_in_2, w_mlp_out_2,
):
    x = first_block(
        x, rel_bias, ln1_g, w_in, b_gate, w_a, pool_w, pool_scale, w_b, ssd_conv_w, ssd_conv_b,
        ssd_dt_bias, ssd_a_log, ssd_d, ssd_norm_w, w_c, w_o, ln2_g, ffn_w_up, ffn_conv_w,
        ffn_conv_b, ffn_w_down, final_g,
    )
    return second_block(
        x, attn_norm_2, w_in_2, diff_q_norm_2, diff_k_norm_2, diff_lam_q1_2, diff_lam_k1_2,
        diff_lam_q2_2, diff_lam_k2_2, diff_subln_2, ret_decay_fwd_2, ret_decay_bwd_2,
        ret_group_norm_2, gqa_q_norm_2, gqa_k_norm_2, w_branch_2, w_out_2, mlp_norm_2,
        w_mlp_in_2, w_mlp_out_2,
    )


_drawn_inputs = setup_inputs


def setup_inputs(seed=0):
    import zlib

    import numpy as np

    out = dict(_drawn_inputs(seed))
    spreads = {}
    factors = {'rel_bias': 6.15,
     'b_gate': 7.565,
     'ssd_norm_w': 3.881,
     'ln2_g': 3.208,
     'diff_q_norm_2': 7.439,
     'diff_k_norm_2': 7.219,
     'diff_lam_q2_2': 7.441,
     'diff_subln_2': 5.392,
     'ret_group_norm_2': 7.407,
     'gqa_q_norm_2': 8.0,
     'gqa_k_norm_2': 8.0}
    for name, (base, spread) in spreads.items():
        noise = np.random.default_rng([zlib.crc32(name.encode()), seed]).standard_normal(out[name].shape)
        drawn = base * np.exp(spread * noise) if base else spread * noise
        out[name] = __import__('jax').numpy.asarray(drawn.astype(out[name].dtype))
    for name, factor in factors.items():
        out[name] = (out[name] * factor).astype(out[name].dtype)
    return out
```

```python
import numpy as np
import concourse.bass as bass
from concourse import mybir

F32 = mybir.dt.float32
F32R = mybir.dt.float32r
ALU = mybir.AluOpType
ACT = mybir.ActivationFunctionType
AX = mybir.AxisListType.X
ds = bass.ds

P = 128
S = 512
D = 1024
KD = D // P
NT = S // P
EPS = 1e-6
CH = 2048
NEG = -1.0e30

HG = 6
HD = 64
DIL = (1, 4, 16)
GW = HG * HD
AW = 3 * GW
POOL0 = 3 * AW
Z0 = POOL0 + D
XBC0 = Z0 + D
XBC = D + 512
DT0 = XBC0 + XBC
GATE0 = DT0 + 16
POOLW = (2, 4, 8, 16)
FF = 2816
FR = FF // 2 // P
LAYERS = 2
FF2 = 4096
MR = 16
COL2 = dict(dq=0, dk=512, dv=1024, rq=1536, rk=2048, rv=2560, rg=3072, gq=3584, gk=4096, gv=4224, gate=4352)
LINE = 384


CN = {}


def const_pack():
    cols = []

    def put(name, a):
        CN[name] = (sum(c.shape[1] for c in cols), a.shape[1])
        full = np.zeros((P, a.shape[1]), np.float32)
        full[:a.shape[0]] = a
        cols.append(full)

    i = np.arange(P)
    put("ident", np.eye(P))
    put("ones", np.ones((P, P)))
    put("blk64", (i[:, None] // 64 == i[None] // 64).astype(np.float32))

    def rot(n, half, block):
        r = np.zeros((P, P))
        for b in range(0, P, block):
            for j in range(half):
                r[b + j, b + j + half] = -1.0
                r[b + j + half, b + j] = 1.0
        return r.T
    put("rot_d", rot(16, 8, 64))
    put("rot_r", rot(128, 64, 128))
    put("rot_g", rot(32, 16, 32))
    put("le", (i[:, None] <= i[None]).astype(np.float32))
    put("gt", (i[:, None] > i[None]).astype(np.float32))
    pos = np.arange(16) + 1
    put("eps", np.tile(np.array([[EPS, 1e-5]]), (P, 1)))
    put("edge", np.tile(np.concatenate([w / np.minimum(pos, w) for w in POOLW])[None], (P, 1)))
    first = np.concatenate(cols, axis=1)
    cols.clear()
    put("mask32", np.where(i[:, None] // 32 == i[None] // 32, 0.0, NEG))
    sel = np.zeros((HG, GW))
    for h in range(HG):
        sel[h, h * HD:(h + 1) * HD] = 1.0
    put("sel", sel)
    for d in DIL:
        rel = 255 - np.arange(LINE)
        ok = (rel >= 0) & (rel <= 128)
        dist = np.clip(rel, 0, None) * d
        nf = np.maximum(dist, 1).astype(np.float32)
        large = 16 + (np.log(nf / np.float32(16)) / np.float32(np.log(128.0)) * np.float32(16)).astype(np.int32)
        bucket = np.where(dist < 16, dist, np.minimum(large, 31))
        oh = np.zeros((33, LINE))
        oh[bucket[ok], np.arange(LINE)[ok]] = 1.0
        oh[32] = np.where(ok, 0.0, NEG)
        put(f"oh{d}", oh)
    second = np.concatenate(cols, axis=1)
    return [np.ascontiguousarray(a.astype(np.float32)) for a in (first, second)]


CONSTS, ATTN_CONSTS = const_pack()


def rope_pack():
    def table(pos, dim, theta):
        inv = (theta ** (-np.arange(0, dim, 2) / dim)).astype(np.float32)
        return (pos.astype(np.float32)[None, :] * inv[:, None]).astype(np.float32).astype(np.float64)
    t = np.arange(S)
    out = np.zeros((3, P, 2, S))
    out[0, :, 0] = 1.0
    a = table(t, 16, 500000.0)
    for b in (0, 64):
        out[0, b:b + 16, 0] = np.cos(np.concatenate([a, a]))
        out[0, b:b + 16, 1] = np.sin(np.concatenate([a, a]))
    a = table(t, 128, 10000.0)
    out[1, :, 0], out[1, :, 1] = np.cos(np.concatenate([a, a])), np.sin(np.concatenate([a, a]))
    for b in (0, 64):
        for o, q in ((0, t // 64), (32, t % 64)):
            a = table(q, 32, 10000.0)
            out[2, b + o:b + o + 32, 0] = np.cos(np.concatenate([a, a]))
            out[2, b + o:b + o + 32, 1] = np.sin(np.concatenate([a, a]))
    return np.ascontiguousarray(out.reshape(3, P, 2 * S).astype(np.float32))


DSTW = S + 3 * P


def dist_pack():
    d = np.arange(DSTW)[None] - 3 * P - np.arange(P)[:, None]
    return np.ascontiguousarray(np.concatenate([np.maximum(d, 0), np.maximum(-d, 0)], axis=1).astype(np.float32))


class Order:

    def __init__(self, slots, before=None):
        self.slots = slots
        self.base_uses = list(before.uses) if before else [0] * slots
        self.base = before.count if before else 0
        self.uses, self.count, self.k, self.names = list(self.base_uses), self.base, 0, {}

    def add(self, *name):
        assert name not in self.names, name
        slot = self.k % self.slots
        self.names[name] = (slot, self.uses[slot], self.count)
        self.uses[slot] += 1
        self.count += 1
        self.k += 1

    def slot(self, name):
        return self.names[name][0]

    def used(self, name, l=0, i=0, n=0):
        slot, uses, _ = self.names[name]
        assert n % self.slots == 0
        return uses + l * (self.uses[slot] - self.base_uses[slot]) + i * (n // self.slots)

    def nth(self, name, l=0, i=0, n=0):
        return self.names[name][2] + 1 + l * (self.count - self.base) + i * n


def order_block1():
    C, G, M = Order(2), Order(4), Order(4)
    for g in range(3):
        M.add("bias", g, 0), M.add("bias", g, 1), M.add("bias", g, 2), M.add("bias", g, 3), M.add("bias", g, 4), M.add("bias", g, 5)
    for i in range(5):
        M.add("par", i)
    for k in range(KD):
        M.add("xT", k)
    M.add("nrm", 0)
    for g in range(3):
        for j in range(5):
            C.add("qkv", g, j)
        for j in range(10 if g < 2 else 9):
            G.add("qkv", g, j)
        if g == 2:
            for t in range(NT):
                M.add("vt", t)
        for h in range(HG + 1):
            if h < HG:
                for b in range(2 if g == 0 else 1):
                    M.add("s", g, h, b)
            if h > 0:
                for b in range(2 if g == 0 else 1):
                    M.add("t", g, h - 1, b)
                M.add("o", g, h - 1)
        for m in range(3):
            M.add("oT", g, m)
        M.add("lT", g)
    for m in range(3):
        for g in range(3):
            M.add("al", m, g)

    def merge(n):
        for j in range(4):
            C.add("g", n, j), C.add("y", n, j)
            for t in range(2):
                G.add("g", n, j, t)
            for t in range(2):
                G.add("y", n, j, t)
    merge(0)
    for j in range(4):
        C.add("pin", j)
        G.add("pin", j, 0), G.add("pin", j, 1)
    C.add("pw")
    for m in range(8):
        G.add("pw", m)
    merge(1)
    C.add("dt")
    G.add("dt")
    for j in range(6):
        C.add("xbc", j)
        G.add("xbc", j, 0), G.add("xbc", j, 1)
    for g in range(2):
        M.add("bt", g)
    for c in range(4):
        M.add("xt", c, 0), M.add("xt", c, 1)
    for c in range(4):
        M.add("ac", c), M.add("cb", c)
        for q in range(4):
            M.add("seg", c, q)
            if q == 1 or q == 3:
                M.add("yd", c, q // 2)
                if c > 0:
                    M.add("yo", c, q // 2)
                if c < 3:
                    M.add("st", c, q // 2)
        M.add("yT", c, 0), M.add("yT", c, 1)
    for j in range(4):
        C.add("z", j)
        G.add("z", j, 0), G.add("z", j, 1)
    M.add("yn", 0), M.add("yn", 1)
    merge(2)
    for j in range(4):
        C.add("wo", j)
        G.add("wo", j, 0), G.add("wo", j, 1)
    M.add("nrm", 1)
    for r in range(2):
        for j in range(FR):
            C.add("up", r, j)
            G.add("up", r, j, 0), G.add("up", r, j, 1)
        for j in range(KD):
            C.add("dn", r, j)
            G.add("dn", r, j)
    M.add("nrm", 2)
    return C, G, M


def order_layer(c1, g1, m1):
    C, G, M = Order(2, c1), Order(4, g1), Order(4, m1)
    C.k = c1.k
    M.add("nrm", 0)

    def merge(n):
        for j in range(4):
            C.add("g", n, j), C.add("y", n, j)
            for t in range(2):
                G.add("g", n, j, t)
            for t in range(2):
                G.add("y", n, j, t)

    def roped(kind, tiles, norm):
        for t in range(tiles + 1):
            if t < tiles:
                if t % 2 == 0:
                    C.add(kind, t // 2)
                G.add(kind, t)
            if 0 < t <= tiles:
                if norm:
                    M.add("ss", kind, t - 1)
                M.add("rot", kind, t - 1)

    def vproj(kind, n):
        for j in range(n):
            C.add(kind, j)
            for t in range(NT):
                G.add(kind, j, t)

    vproj("dv", 2)
    roped("d", 8, True)
    for u in range(20):
        if u < 16:
            G.add("s", u, 0), G.add("s", u, 1)
        if 2 <= u < 18:
            M.add("t", u - 2)
        if u >= 6 and u % 4 == 2:
            M.add("pv", u // 4 - 1)
        if u >= 7 and u % 4 == 3:
            M.add("on", u // 4 - 1)
    merge(0)
    vproj("rv", 2)
    roped("r", 8, False)
    for j in range(2):
        C.add("rg", j)
        G.add("rg", j, 0), G.add("rg", j, 1)
    for h in range(5):
        if h < 4:
            for j in range(4):
                G.add("rs", h, j)
        if h > 0:
            M.add("rm", h - 1)
        if h < 4:
            M.add("ro", h)
        if h > 0:
            M.add("rn", h - 1)
    merge(1)
    vproj("gv", 1)
    roped("g", 6, True)
    for u in range(35):
        if u < 32:
            G.add("gs", u)
        if 2 <= u < 34:
            M.add("gt", u - 2)
        if u >= 6 and u % 4 == 2:
            M.add("gpv", u // 4 - 1)
    merge(2)
    for j in range(4):
        C.add("wo", j)
        G.add("wo", j, 0), G.add("wo", j, 1)
    M.add("nrm", 1)
    for r in range(2):
        for j in range(KD):
            C.add("up", r, j)
            G.add("up", r, j, 0), G.add("up", r, j, 1)
        for j in range(KD):
            C.add("dn", r, j)
            G.add("dn", r, j)
    return C, G, M


C1, G1, M1 = order_block1()
C2, G2, M2 = order_layer(C1, G1, M1)
assert (C2.count - C2.base) % 2 == 0


class Steps:

    def __init__(self, eng, sem):
        self.e, self.sem, self.n, self.L, self.dirty, self.pend = eng, sem, 0, 0, False, []

    def s(self, ins):
        ins.then_inc(self.sem, 1)
        self.n += 1
        self.dirty = True

    def f(self, ins, sem, val):
        ins.then_inc(sem, 1)
        self.pend.append((sem, val))

    def w(self):
        if self.dirty:
            self.e.wait_ge(self.sem, self.n + self.L)
        for sem, val in self.pend:
            self.e.wait_ge(sem, val)
        self.dirty, self.pend = False, []

    def loop(self, count, incs, body):
        n0, L0, pend = self.n, self.L, self.pend
        with self.e.Fori(0, count) as i:
            self.L, self.pend, self.dirty = L0 + i * incs, list(pend), n0 > 0
            self.w()
            body(i)
            self.w()
        assert self.n - n0 == incs, f"this loop's body takes {self.n - n0} steps, not {incs}"
        self.n, self.L = n0 + incs * count, L0


def build(nc, a, out, consts, attn_consts, ropes, dists, line_dram):
    BASE = 16512
    top = nc.sbuf_usable_end

    def at(name, shape, dt, off):
        return nc.alloc_sbuf_tensor_at(name, shape, dt, offset=off)

    fence = nc.alloc_sbuf_tensor("fence", [P, (top - BASE - 64) // 4], F32)
    hT = at("hT", [P, KD, S], F32, BASE)
    uH = at("uH", [P, KD, S], F32R, BASE + 16384)
    uL = at("uL", [P, KD, S], F32R, BASE + 32768)
    mg = at("mg", [P, KD, S], F32, BASE + 49152)
    wR = at("wR", [P, 2, CH], F32, BASE + 65536)
    wH = at("wH", [P, 2, CH], F32R, BASE + 81920)
    wL = at("wL", [P, 2, CH], F32R, BASE + 98304)
    Z = BASE + 114688
    bH = at("bH", [P, KD, S], F32R, Z)
    bL = at("bL", [P, KD, S], F32R, Z + 16384)
    mH = at("mH", [P, MR, S], F32R, Z)
    mL = at("mL", [P, MR, S], F32R, Z + 32768)
    WK = Z + 32768
    END = (top - 64) // 128 * 128
    cn = at("cn", [P, CONSTS.shape[1]], F32, END - 8192)
    PT = at("PT", [P, 4, P], F32, END - 3712)
    lay = at("lay", [P, 2, 16], F32, END - 1664)
    lp = at("lp", [P, 64], F32, END - 1536)
    nrmt = at("nrmt", [P, S], F32, END - 8192 - 2048)
    sg = at("sg", [P, 2, S], F32, END - 8192 - 2048 - 4096)
    WEND = END - 14336
    assert (WEND - WK) >= 50000, WEND - WK

    class Work:

        def __init__(self, start, end):
            self.o, self.end = start, end

        def get(self, name, shape, dt=F32):
            n = 4 * int(np.prod(shape[1:]))
            n += -n % 32
            t = at(name, shape, dt, self.o)
            self.o += n
            assert self.o <= self.end, (name, self.o - self.end)
            return t

    def C(name, rows=P):
        o, n = CN[name]
        return cn[0:rows, o:o + n]

    ps = [nc.alloc_psum_tensor(f"ps{b}", [P, S], F32) for b in range(8)]
    sems = {}

    def sem(name):
        if name not in sems:
            sems[name] = nc.alloc_semaphore(name)
        return sems[name]

    gemm_ready, misc_ready = sem("gemm_ready"), sem("misc_ready")
    gemm_free = [sem(f"gemm_free{b}") for b in range(4)]
    misc_free = [sem(f"misc_free{b}") for b in range(4)]
    raw_ready = [sem(f"raw_ready{b}") for b in range(2)]
    hi_ready, lo_ready = sem("hi_ready"), sem("lo_ready")

    class Grp:
        def __init__(self, order, kind, *name, l=0, i=0, n=0):
            self.slot = order.slot(name)
            self.used, self.nth = order.used(name, l, i, n), order.nth(name, l, i, n)
            self.ready = gemm_ready if kind == "g" else misc_ready
            self.free = (gemm_free if kind == "g" else misc_free)[self.slot]
            self.ps = ps[self.slot + (0 if kind == "g" else 4)]

        def open(self, pe):
            if not (isinstance(self.used, int) and self.used == 0):
                pe.wait_ge(self.free, self.used)
            return self.ps

        def close(self, ins):
            ins.then_inc(self.ready, 1)

        def take(self, e):
            e.wait_ge(self.ready, self.nth)
            return self.ps

        def done(self, st, ins):
            st.f(ins, self.free, self.used + 1)

    def G(*name, l=None, i=0, n=0):
        return Grp(G1, "g", *name, i=i, n=n) if l is None else Grp(G2, "g", *name, l=l, i=i, n=n)

    def M(*name, l=None, i=0, n=0):
        return Grp(M1, "m", *name, i=i, n=n) if l is None else Grp(M2, "m", *name, l=l, i=i, n=n)

    def chunk(name, l, i, n):
        o = C1 if l is None else C2
        l = 0 if l is None else l
        return o.slot(name), o.used(name, l, i, n), o.nth(name, l, i, n)

    def load(e, name, parts, l=None, i=0, n=0):
        slot, used, nth = chunk(name, l, i, n)
        if not (isinstance(nth, int) and nth <= 2):
            e.wait_ge(lo_ready, nth - 2)
            if not isinstance(nth, int):
                e.sem_inc(sem("slot_turns"), 1)
        for dst, src in parts(wR[:, slot, :]):
            e.dma_start(dst, src).then_inc(raw_ready[slot], 16)

    def high(st, name, grp, l=None, i=0, n=0, first=False):
        slot, used, nth = chunk(name, l, i, n)
        ahead = 0 if first else 1
        if not first:
            st.e.wait_ge(grp.ready, grp.nth)
        st.w()
        st.e.wait_ge(raw_ready[slot], (used + ahead + 1) * 32)
        st.f(st.e.activation(wH[:, slot, :], wR[:, slot, :], ACT.Copy), hi_ready, nth + 2 * ahead)

    def low(st, name, l=None, i=0, n=0, first=False):
        slot, used, nth = chunk(name, l, i, n)
        ahead = 0 if first else 1
        st.w()
        st.e.wait_ge(hi_ready, nth + 2 * ahead)
        st.f(st.e.tensor_tensor(wL[:, slot, :], wR[:, slot, :], wH[:, slot, :].bitcast(F32), ALU.subtract),
             lo_ready, nth + 2 * ahead)

    def use(pe, name, l=None, i=0, n=0):
        slot, used, nth = chunk(name, l, i, n)
        pe.wait_ge(lo_ready, nth)
        return slot

    def wk(t, slot, kt, n, off=0):
        return t[:, slot, off:off + kt * n].rearrange("p (k n) -> p k n", k=kt)

    def product(pe, outp, slot, kt, n, c0, m, xH, xL, off=0, start=True, stop=True, tile_ready=None):
        h, lo = wk(wH, slot, kt, n, off), wk(wL, slot, kt, n, off)
        steps = [(w, x, k) for k in range(kt) for w, x in ((h, xH), (h, xL), (lo, xH))]
        for s, (w, x, k) in enumerate(steps):
            if tile_ready and s % 3 == 0:
                pe.wait_ge(*tile_ready(k))
            ins = pe.matmul(outp, w[:, k, c0:c0 + m], x[:, k, :], start=start and s == 0,
                            stop=stop and s == len(steps) - 1)
        return ins

    def product_pair(pe, groups, slot, kt, xH, xL, tile_ready):
        h, lo = wk(wH, slot, kt, 2 * P), wk(wL, slot, kt, 2 * P)
        outs = [g.open(pe) for g in groups]
        for k in range(kt):
            pe.wait_ge(*tile_ready(k))
            for t, (g, o) in enumerate(zip(groups, outs)):
                for s, (w, x) in enumerate(((h, xH), (h, xL), (lo, xH))):
                    ins = pe.matmul(o[:, :], w[:, k, t * P:t * P + P], x[:, k, :], start=k == 0 and s == 0,
                                    stop=k == kt - 1 and s == 2)
                if k == kt - 1:
                    g.close(ins)

    def product_tok(pe, outp, slot, kt, n, cols, uh, ul):
        h, lo = wk(wH, slot, kt, n), wk(wL, slot, kt, n)
        steps = [(w, x, k) for k in range(kt) for w, x in ((h, uh), (h, ul), (lo, uh))]
        for s, (w, x, k) in enumerate(steps):
            ins = pe.matmul(outp, x(k), w[:, k, 0:cols], start=s == 0, stop=s == len(steps) - 1)
        return ins

    def product_tok_all(pe, groups, slot, n, cols, tile_ready):
        h, lo = wk(wH, slot, KD, n), wk(wL, slot, KD, n)
        outs = [g.open(pe) for g in groups]
        for k in range(KD):
            pe.wait_ge(*tile_ready(k))
            for t, (g, o) in enumerate(zip(groups, outs)):
                for s, (w, x) in enumerate(((h, uH), (h, uL), (lo, uH))):
                    ins = pe.matmul(o[:, 0:cols], x[:, k, t * P:(t + 1) * P], w[:, k, 0:cols],
                                    start=k == 0 and s == 0, stop=k == KD - 1 and s == 2)
                if k == KD - 1:
                    g.close(ins)

    def kcols(w, r0, kt, c0, n):
        return w[r0:r0 + kt * P, :].rearrange("(k p) n -> p k n", p=P)[:, :, ds(c0, n) if not isinstance(c0, int) else slice(c0, c0 + n)]

    def by_k(w, kt, n, c0, r0=0):
        def parts(slot):
            d = slot[:, 0:kt * n].rearrange("p (k n) -> p k n", k=kt)
            s, h = kcols(w, r0, kt, c0, n), (kt + 1) // 2
            return [(d[:, 0:h, :], s[:, 0:h, :]), (d[:, h:kt, :], s[:, h:kt, :])]
        return parts

    def by_cols(w, kt, ca, cb, n=P, r0=0):
        def parts(slot):
            d = slot[:, 0:kt * 2 * n].rearrange("p (k n) -> p k n", k=kt)
            return [(d[:, :, 0:n], kcols(w, r0, kt, ca, n)), (d[:, :, n:2 * n], kcols(w, r0, kt, cb, n))]
        return parts

    w1 = a["w_in"][0]
    w2 = a["w_in_2"]

    def nrm_grp(which, l):
        return M("nrm", which, l=l)

    def norm_count(which, l):
        return which if l is None else 3 + 2 * l + which

    def norm_seen(c):
        return 8 * c if isinstance(c, int) and c < 3 else 8 * c - 8

    def norm_act(st, which, l=None):
        e, c = st.e, norm_count(which, l)
        for k in range(KD):
            e.wait_ge(sem("h_ready"), 8 * c + k + 1)
            st.w()
            st.f(e.activation(mg[:, k, :], hT[:, k, :], ACT.Square), sem("square_ready"), 8 * c + k + 1)
        g = nrm_grp(which, l)
        o = g.take(e)
        st.w()
        g.done(st, e.activation(nrmt[:, :], o[:, :], ACT.Sqrt, bias=C("eps")[:, 0:1], scale=1.0 / D))
        st.w()
        e.sem_inc(sem("root_ready"), 1)
        if which == 2:
            return
        for k in range(KD):
            e.wait_ge(sem("normed_ready"), norm_seen(c) + k + 1)
            st.w()
            st.f(e.activation(uH[:, k, :], mg[:, k, :], ACT.Copy), sem("uH_ready"), norm_seen(c) + k + 1)

    def norm_pe(pe, which, l=None):
        c, g = norm_count(which, l), nrm_grp(which, l)
        o = g.open(pe)
        for k in range(KD):
            pe.wait_ge(sem("square_ready"), 8 * c + k + 1)
            ins = pe.matmul(o[:, :], C("ones"), mg[:, k, :], start=k == 0, stop=k == KD - 1)
        g.close(ins)

    def norm_dve(st, which, gains, l=None):
        e, c = st.e, norm_count(which, l)
        e.wait_ge(sem("root_ready"), c + 1)
        st.s(e.reciprocal(nrmt[:, :], nrmt[:, :]))
        st.w()

        def low_part(k):
            e.wait_ge(sem("uH_ready"), norm_seen(c) + k + 1)
            st.w()
            st.f(e.tensor_tensor(uL[:, k, :], mg[:, k, :], uH[:, k, :].bitcast(F32), ALU.subtract),
                 sem("u_ready"), norm_seen(c) + k + 1)
        for k in range(KD):
            if which == 2:
                st.f(e.scalar_tensor_tensor(out=hT[:, k, :], in0=hT[:, k, :], scalar=gains(k), in1=nrmt[:, :],
                                            op0=ALU.mult, op1=ALU.mult), sem("h_ready"), 8 * c + 8 + k + 1)
            else:
                st.f(e.scalar_tensor_tensor(out=mg[:, k, :], in0=hT[:, k, :], scalar=gains(k), in1=nrmt[:, :],
                                            op0=ALU.mult, op1=ALU.mult), sem("normed_ready"), norm_seen(c) + k + 1)
                if k > 0:
                    low_part(k - 1)
        if which == 2:
            st.w()
        else:
            low_part(KD - 1)

    def u_tile(which, l=None):
        return lambda k: (sem("u_ready"), norm_seen(norm_count(which, l)) + k + 1)

    def split_act(st, src, tiles, n, wait=None):
        for k in range(tiles):
            if wait:
                wait(st.e, k)
            st.w()
            st.f(st.e.activation(bH[:, k, :], src(k), ACT.Copy), sem("bH_ready"), n + k + 1)

    def split_dve(st, src, tiles, n):
        for k in range(tiles):
            st.e.wait_ge(sem("bH_ready"), n + k + 1)
            st.w()
            st.f(st.e.tensor_tensor(bL[:, k, :], src(k), bH[:, k, :].bitcast(F32), ALU.subtract), sem("b_ready"), n + k + 1)

    def merge_sp(e, n, wy, kt, gates, l=None):
        def body(i):
            load(e, ("g", n, 0), by_k(gates[0], KD, 2 * P, gates[1] + n * D + i * 2 * P), l, i, 2)
            load(e, ("y", n, 0), by_k(wy, kt, 2 * P, i * 2 * P), l, i, 2)
        with e.Fori(0, 4) as i:
            body(i)

    def merge_pe(pe, n, kt, count, l=None):
        with pe.Fori(0, 4) as i:
            slot = use(pe, ("g", n, 0), l, i, 2)
            for t in range(2):
                g = G("g", n, 0, t, l=l, i=i, n=4)
                o = g.open(pe)
                g.close(product(pe, o[:, :], slot, KD, 2 * P, t * P, P, uH, uL))
            slot = use(pe, ("y", n, 0), l, i, 2)
            product_pair(pe, [G("y", n, 0, t, l=l, i=i, n=4) for t in range(2)], slot, kt, bH, bL,
                         lambda k: (sem("b_ready"), count - kt + k + 1))

    def merge_count(n, l):
        return (8 * n if l is None else 24 + 24 * l + 8 * n)

    def merge_act(st, n, l=None):
        e, m0 = st.e, merge_count(n, l)

        def body(i):
            for t in range(2):
                g = G("g", n, 0, t, l=l, i=i, n=4)
                if t == 1:
                    high(st, ("g", n, 0), g, l, i, 2)
                o = g.take(e)
                e.wait_ge(sem("sg_free"), 2 + m0 + 2 * i)
                st.w()
                bias = PT[:, 0, ds(8 + n * 8 + 2 * i + t, 1)] if l is None else 0.0
                g.done(st, e.activation(sg[:, t, :], o[:, :], ACT.Sigmoid, bias=bias))
                st.w()
                e.sem_inc(sem("sg_ready"), 1)
            high(st, ("y", n, 0), G("y", n, 0, 1, l=l, i=i, n=4), l, i, 2)
        st.loop(4, 0, body)

    def merge_dve(st, n, l=None):
        e, m0 = st.e, merge_count(n, l)

        def body(i):
            low(st, ("g", n, 0), l, i, 2)
            for t in range(2):
                if t == 1:
                    low(st, ("y", n, 0), l, i, 2)
                g = G("y", n, 0, t, l=l, i=i, n=4)
                o = g.take(e)
                e.wait_ge(sem("sg_ready"), m0 + 2 * i + t + 1)
                tile = mgf[:, ds((2 * i + t) * S, S)]
                st.w()
                if n == 0:
                    g.done(st, e.tensor_tensor(tile, o[:, :], sg[:, t, :], ALU.mult))
                else:
                    g.done(st, e.tensor_tensor(sg[:, t, :], o[:, :], sg[:, t, :], ALU.mult))
                    st.w()
                    st.s(e.tensor_tensor(tile, tile, sg[:, t, :], ALU.add))
                st.w()
                e.sem_inc(sem("sg_free"), 1)
        st.loop(4, 0 if n == 0 else 2, body)

    mgf = mg[:, :, :].rearrange("p k s -> p (k s)")
    hTf = hT[:, :, :].rearrange("p k s -> p (k s)")

    def out_sp(e, w, l=None):
        with e.Fori(0, 2) as i:
            for j in range(2):
                load(e, ("wo", j), by_k(w, KD, 2 * P, i * 4 * P + j * 2 * P), l, i, 2)

    def out_pe(pe, count, l=None):
        with pe.Fori(0, 2) as i:
            for j in range(2):
                slot = use(pe, ("wo", j), l, i, 2)
                if j == 0:
                    product_pair(pe, [G("wo", j, t, l=l, i=i, n=4) for t in range(2)], slot, KD, bH, bL,
                                 lambda k: (sem("b_ready"), count - KD + k + 1))
                    continue
                for t in range(2):
                    g = G("wo", j, t, l=l, i=i, n=4)
                    o = g.open(pe)
                    g.close(product(pe, o[:, :], slot, KD, 2 * P, t * P, P, bH, bL))

    def out_act(st, l=None):
        def body(i):
            for j in range(2):
                high(st, ("wo", j), G("wo", j, 1, l=l, i=i, n=4), l, i, 2)
        st.loop(2, 0, body)

    def out_dve(st, l=None):
        e = st.e

        def body(i):
            for j in range(2):
                for t in range(2):
                    g = G("wo", j, t, l=l, i=i, n=4)
                    o = g.take(e)
                    tile = hTf[:, ds((4 * i + 2 * j + t) * S, S)]
                    st.w()
                    g.done(st, e.tensor_tensor(tile, tile, o[:, :], ALU.add))
                    st.w()
                    e.sem_inc(sem("h_ready"), 1)
                low(st, ("wo", j), l, i, 2)
        st.loop(2, 0, body)

    sw = Work(WK, WEND)
    xin = sw.get("xin", [P, NT, D])
    prow = sw.get("prow", [P, 4, P])
    lamv = sw.get("lamv", [P, LAYERS, 4, HD])
    decv = sw.get("decv", [P, LAYERS, 2, 4])
    dskip = sw.get("dskip", [P, 2])
    lams = sw.get("lams", [P, LAYERS, 4, HD])
    acn = at("acn", [P, ATTN_CONSTS.shape[1]], F32, BASE + 16384)
    tabx = at("tabx", [33, 3 * HG, P], F32, BASE + 32768)
    lines = at("lines", [P, 6, LINE], F32, BASE + 16384 + 6656)
    tab = at("tab", [33, 3 * HG], F32, BASE + 32768 + 9216)

    def AC(name, rows=P):
        o, n = CN[name]
        return acn[0:rows, o:o + n]

    par = [("ln1_g", 0, 0, 8), ("b_gate", 0, 8, 24), ("pool_scale", 0, 32, 8), ("ssd_conv_b", 0, 88, 12),
           ("ssd_norm_w", 0, 100, 8), ("ln2_g", 0, 108, 8), ("ffn_conv_b", 2, 44, 44)]
    PROWS = [124, 88, 120, 18]

    def setup_sp(e):
        e.dma_start(cn[:, :], consts).then_inc(sem("const_in"), 16)
        xr = a["x"][0].rearrange("(t p) d -> p t d", p=P)
        for t in range(NT):
            e.dma_start(xin[:, t, :], xr[:, t, :]).then_inc(sem("x_in"), 16)

    def setup_pool(e):
        st = Steps(e, sem("pool_step"))
        n = [0]

        def dma(dst, src):
            e.dma_start(dst, src).then_inc(sem("par_in"), 16)
            n[0] += 16
        for name, pack, row, rows in par:
            dma(prow[row:row + rows, pack, :], a[name][0].rearrange("(k p) -> k p", p=P))
        dma(prow[116:124, 0, :], a["final_g"].rearrange("(k p) -> k p", p=P))
        dma(prow[40:88, 0, :], a["ssd_conv_w"][0].rearrange("t (k p) -> (t k) p", p=P))
        dma(prow[0:88, 1, :], a["ffn_conv_w"][0, 0:2].rearrange("t (k p) -> (t k) p", p=P))
        dma(prow[0:44, 2, :], a["ffn_conv_w"][0, 2].rearrange("(k p) -> k p", p=P))
        dma(dskip[32:40, :], a["ssd_d"][0].rearrange("(k h) -> k h", h=2))
        dma(prow[88:104, 2, :], a["attn_norm_2"].rearrange("l (k p) -> (l k) p", p=P))
        dma(prow[104:120, 2, :], a["mlp_norm_2"].rearrange("l (k p) -> (l k) p", p=P))
        for l in range(LAYERS):
            for j, name in enumerate(("diff_q_norm_2", "diff_k_norm_2", "gqa_q_norm_2", "gqa_k_norm_2")):
                for h in range(2):
                    dma(prow[9 * l + j:9 * l + j + 1, 3, h * 64:h * 64 + 64], a[name][l:l + 1, :])
            dma(prow[9 * l + 4:9 * l + 5, 3, :], a["diff_subln_2"][l:l + 1, :])
            dma(prow[9 * l + 5:9 * l + 9, 3, :], a["ret_group_norm_2"][l].rearrange("(k p) -> k p", p=P))
            for j, name in enumerate(("diff_lam_q1_2", "diff_lam_k1_2", "diff_lam_q2_2", "diff_lam_k2_2")):
                dma(lamv[:, l, j, :], a[name][l].partition_broadcast(P))
            for j, name in enumerate(("ret_decay_fwd_2", "ret_decay_bwd_2")):
                dma(decv[:, l, j, :], a[name][l].partition_broadcast(P))
        setup_pool.count = n[0]
        e.dma_start(acn[:, :], attn_consts).then_inc(sem("acn_in"), 16)
        e.memset(tab[32:33, :], 1.0).then_inc(sem("pool_step"), 1)
        e.dma_start(tab[0:32, :], a["rel_bias"]).then_inc(sem("acn_in"), 16)
        for g in range(3):
            e.wait_ge(sem("lines_ready"), 6 * (g + 1))
            e.dma_start(line_dram[HG * g:HG * g + HG].rearrange("h p y -> p h y"), lines[:, :, :]).then_inc(sem("lines_out"), 16)

    PAR_DMAS = 16 * (len(par) + 4 + 1 + 2 + LAYERS * (8 + 2 + 4 + 2))

    def setup_dve(st):
        e = st.e
        e.sem_inc(sem("sg_free"), 2)
        e.wait_ge(sem("acn_in"), 32)
        e.wait_ge(sem("pool_step"), 1)
        st.s(e.tensor_copy(tabx[:, :, :], tab[:, :].unsqueeze(2).broadcast_to([33, 3 * HG, P])))
        st.w()
        e.sem_inc(sem("tabx_ready"), 1)
        e.wait_ge(sem("par_in"), PAR_DMAS)
        st.s(e.tensor_copy(prow[32:40, 3, :].rearrange("p (h d) -> p h d", h=2), dskip[32:40, :].unsqueeze(2).broadcast_to([8, 2, HD])))
        st.w()
        e.sem_inc(sem("dskip_ready"), 1)
        for i in range(4):
            g = M("par", i)
            o = g.take(e)
            g.done(st, e.tensor_copy(PT[:, i, 0:PROWS[i]], o[:, 0:PROWS[i]]))
        g = M("par", 4)
        o = g.take(e)
        g.done(st, e.tensor_copy(PT[:, 3, 32:40], o[:, 0:8]))
        st.w()
        e.sem_inc(sem("PT_ready"), 1)
        e.wait_ge(sem("par_in"), PAR_DMAS)
        for l in range(LAYERS):
            for j in range(2):
                st.s(e.tensor_tensor(lams[:, l, j, :], lamv[:, l, 2 * j, :], lamv[:, l, 2 * j + 1, :], ALU.mult))
        st.w()
        for l in range(LAYERS):
            st.s(e.tensor_reduce(lay[:, l, 9:11], lams[:, l, 0:2, :], AX, ALU.add))
        st.w()
        e.sem_inc(sem("lam_dots"), 1)
        e.wait_ge(sem("lam_exps"), 4)
        for l in range(LAYERS):
            init = 0.8 - 0.6 * float(np.exp(-0.3 * l))
            st.s(e.tensor_tensor(lay[:, l, 0:1], lay[:, l, 10:11], lay[:, l, 9:10], ALU.subtract))
            st.w()
            st.s(e.tensor_scalar(lay[:, l, 0:1], lay[:, l, 0:1], -init, None, ALU.add))
            st.s(e.tensor_scalar(lay[:, l, 1:9], lay[:, l, 1:9], -1.0, None, ALU.mult))
            st.s(e.tensor_scalar(PT[:, 3, 9 * l + 4:9 * l + 5], PT[:, 3, 9 * l + 4:9 * l + 5], 1.0 - init, None, ALU.mult))
        st.w()
        for k in range(KD):
            g = M("xT", k)
            o = g.take(e)
            g.done(st, e.tensor_copy(hT[:, k, :], o[:, :]))
            st.w()
            e.sem_inc(sem("h_ready"), 1)

    def setup_act(st):
        e = st.e
        for g3 in range(3):
            for h in range(HG):
                g = M("bias", g3, h)
                o = g.take(e)
                if g3:
                    e.wait_ge(sem("lines_out"), 16 * g3)
                st.w()
                g.done(st, e.activation(lines[:, h, :], o[:, 0:LINE], ACT.Copy))
                st.w()
                e.sem_inc(sem("lines_ready"), 1)
        e.wait_ge(sem("lam_dots"), 1)
        for l in range(LAYERS):
            st.f(e.activation(lay[:, l, 9:11], lay[:, l, 9:11], ACT.Exp), sem("lam_exps"), 2 * l + 1)
            e.wait_ge(sem("par_in"), PAR_DMAS)
            st.f(e.activation(lay[:, l, 1:9], decv[:, l, :, :].rearrange("p a b -> p (a b)"), ACT.Exp), sem("lam_exps"), 2 * l + 2)
        st.w()

    def setup_pe(pe):
        pe.wait_ge(sem("const_in"), 16)
        pe.wait_ge(sem("acn_in"), 32)
        pe.wait_ge(sem("tabx_ready"), 1)
        for g3 in range(3):
            for h in range(HG):
                g = M("bias", g3, h)
                o = g.open(pe)
                g.close(pe.matmul(o[:, 0:LINE], tabx[:, HG * g3 + h, :], AC(f"oh{DIL[g3]}", 33), start=True, stop=True))
        pe.wait_ge(sem("par_in"), PAR_DMAS)
        for i in range(4):
            g = M("par", i)
            o = g.open(pe)
            n = PROWS[i]
            g.close(pe.transpose(o[:, 0:n], prow[0:n, i, :], C("ident")[0:n, 0:n]))
        pe.wait_ge(sem("dskip_ready"), 1)
        g = M("par", 4)
        o = g.open(pe)
        g.close(pe.transpose(o[:, 0:8], prow[32:40, 3, :], C("ident")[32:40, 32:40]))
        pe.wait_ge(sem("x_in"), 16 * NT)
        for k in range(KD):
            g = M("xT", k)
            o = g.open(pe)
            for t in range(NT):
                ins = pe.transpose(o[:, t * P:(t + 1) * P], xin[:, t, k * P:(k + 1) * P], C("ident"))
            g.close(ins)

    aw = Work(WK, WEND)
    qT = aw.get("qT", [P, 3, S])
    kT = aw.get("kT", [P, 3, S])
    vt = aw.get("vt", [P, NT, GW])
    sc = aw.get("sc", [P, 2, 4 * 256])
    vT = at("vT", [P, 3, S], F32, WK + 3 * 6144)
    pT = aw.get("pT", [P, 2, 8 * P])
    oTx = aw.get("oTx", [P, S])
    msk = aw.get("msk", [P, P + GW])
    stat = aw.get("stat", [P, 6, 4, HG])
    otok = at("otok", [P, NT, GW], F32, Z + 6144)
    biasT = at("biasT", [P, HG, 256], F32, Z + 16384 + 6144)
    lT = aw.get("lT", [HG, 3, S])
    lx = aw.get("lx", [HG, 2, S])

    def perm(ap, d):
        return ap.rearrange("p (i r) -> p r i", r=d)

    def res(ap, d):
        return ap.rearrange("p (r i) -> p r i", r=d)

    def group_out(g, m):
        n = 3 * g + m
        return mg[:, n, :] if n < 8 else oTx[:, :]

    def attn_sp(e):
        for g in range(3):
            q0, k0, v0 = g * GW, AW + g * GW, 2 * AW + g * GW
            load(e, ("qkv", g, 0), by_cols(w1, KD, q0, q0 + P))
            load(e, ("qkv", g, 1), by_cols(w1, KD, q0 + 2 * P, k0))
            load(e, ("qkv", g, 2), by_cols(w1, KD, k0 + P, k0 + 2 * P))
            load(e, ("qkv", g, 3), by_k(w1, KD, 2 * P, v0))
            load(e, ("qkv", g, 4), by_k(w1, KD, P, v0 + 2 * P))

    def attn_pool(e):
        e.wait_ge(sem("h_ready"), 8)
        e.dma_start(msk[:, 0:P], attn_consts[:, 0:P]).then_inc(sem("msk_in"), 16)
        e.dma_start(msk[:, P:P + GW], attn_consts[:, CN["sel"][0]:CN["sel"][0] + GW]).then_inc(sem("msk_in"), 16)
        e.wait_ge(sem("lines_out"), 48)
        for g in range(3):
            if g:
                e.wait_ge(sem("bias_used"), g)
            for h in range(HG):
                base = line_dram[HG * g + h]
                src = bass.AP(tensor=base.tensor, offset=base.offset + 127, ap=[[LINE - 1, P], [1, 256]])
                e.dma_start(biasT[:, h, :], src).then_inc(sem("bias_in"), 16)

    def attn_pe(pe):
        for g in range(3):
            d = DIL[g]
            for j in range(3):
                slot = use(pe, ("qkv", g, j))
                if g == 0 and j == 0:
                    product_pair(pe, [G("qkv", g, t) for t in range(2)], slot, KD, uH, uL, u_tile(0))
                    continue
                for t in range(2):
                    gr = G("qkv", g, 2 * j + t)
                    o = gr.open(pe)
                    gr.close(product(pe, o[:, :], slot, KD, 2 * P, t * P, P, uH, uL))
            if g == 2:
                for j, t in ((3, 0), (3, 1), (4, 0)):
                    if t == 0:
                        slot = use(pe, ("qkv", g, j))
                    gr = G("qkv", g, 2 * j + t)
                    o = gr.open(pe)
                    gr.close(product(pe, o[:, :], slot, KD, 2 * P if j == 3 else P, t * P, P, uH, uL))
                pe.wait_ge(sem("vT_ready"), 3)
                for t in range(NT):
                    gr = M("vt", t)
                    o = gr.open(pe)
                    for m in range(3):
                        ins = pe.transpose(o[:, m * P:(m + 1) * P], vT[:, m, t * P:(t + 1) * P], C("ident"))
                    gr.close(ins)
            grs = [G("qkv", g, 6 + t) for t in range(NT)] if g < 2 else []
            for j, (c0, cols) in enumerate(((0, 2 * P), (2 * P, P)) if g < 2 else ()):
                slot = use(pe, ("qkv", g, 3 + j))
                for t in range(NT):
                    o = grs[t].open(pe) if j == 0 else grs[t].ps
                    if d == 1:
                        uh, ul = (lambda k: uH[:, k, t * P:(t + 1) * P]), (lambda k: uL[:, k, t * P:(t + 1) * P])
                    else:
                        uh, ul = (lambda k: uH[:, k, t:S:d]), (lambda k: uL[:, k, t:S:d])
                    ins = product_tok(pe, o[:, c0:c0 + cols], slot, KD, cols, cols, uh, ul)
                    if j == 1:
                        grs[t].close(ins)

            def scores(h):
                hp, ht = HD * (h % 2), h // 2
                q, k = qT[hp:hp + HD, ht, :], kT[hp:hp + HD, ht, :]
                if h == 0:
                    pe.wait_ge(sem("qk_ready"), 6 * (g + 1))
                for b in range(2 if g == 0 else 1):
                    gr = M("s", g, h, b)
                    o = gr.open(pe)
                    for n in ((2 * b, 2 * b + 1) if g == 0 else range(4)):
                        if g == 0:
                            k0 = max(n - 1, 0) * P
                            c = 256 * (n % 2) + (P if n == 0 else 0)
                            ins = pe.matmul(o[:, c:c + (n + 1) * P - k0], q[:, n * P:(n + 1) * P], k[:, k0:(n + 1) * P],
                                            start=True, stop=True)
                        else:
                            ins = pe.matmul(o[:, n * P:(n + 1) * P], q[:, n * P:(n + 1) * P], k[:, n * P:(n + 1) * P],
                                            start=True, stop=True)
                    gr.close(ins)

            def weighted(h):
                u = 6 * g + h
                pe.wait_ge(sem("prob_ready"), u + 1)
                blocks = KEYS[g]
                for b in range(len(blocks) // 4 + (len(blocks) % 4 > 0)):
                    gr = M("t", g, h, b)
                    o = gr.open(pe)
                    for x, (n, kt, c) in enumerate(blocks[4 * b:4 * b + 4]):
                        ins = pe.transpose(o[:, x * P:(x + 1) * P], sc[:, u % 2, c:c + P], C("ident"))
                    gr.close(ins)
                pe.wait_ge(sem("pT_ready"), u + 1)
                if u == 6 * g:
                    pe.wait_ge(sem("v_ready"), 4 * (g + 1))
                gr = M("o", g, h)
                o = gr.open(pe)
                for n in range(4):
                    mine = [(x, kt) for x, (m, kt, c) in enumerate(blocks) if m == n]
                    for y, (x, kt) in enumerate(mine):
                        ins = pe.matmul(o[:, n * HD:(n + 1) * HD], pT[:, u % 2, x * P:(x + 1) * P],
                                        vt[:, kt, h * HD:(h + 1) * HD], start=y == 0, stop=y == len(mine) - 1)
                gr.close(ins)

            for h in range(HG + 1):
                if h < HG:
                    scores(h)
                if h > 0:
                    weighted(h - 1)
            pe.wait_ge(sem("otok_ready"), 6 * (g + 1))
            for m in range(3):
                gr = M("oT", g, m)
                o = gr.open(pe)
                for n in range(NT):
                    ins = pe.transpose(o[:, n * P:(n + 1) * P], otok[:, n, m * P:(m + 1) * P], C("ident"))
                gr.close(ins)
            pe.wait_ge(sem("lse_ready"), g + 1)
            gr = M("lT", g)
            o = gr.open(pe)
            for n in range(NT):
                ins = pe.transpose(o[0:HG, n * P:(n + 1) * P], stat[:, 4, n, :], C("ident"))
            gr.close(ins)
        pe.wait_ge(sem("alpha_ready"), 1)
        for m in range(3):
            for g in range(3):
                gr = M("al", m, g)
                o = gr.open(pe)
                gr.close(pe.matmul(o[:, :], msk[0:HG, P + m * P:P + (m + 1) * P], lT[:, g, :], start=True, stop=True))

    KEYS = [[(n, kt, 256 * n + P * (kt - n + 1)) for n in range(4) for kt in (n - 1, n) if kt >= 0]] + \
           [[(n, n, P * n) for n in range(4)]] * 2

    def attn_act(st):
        e = st.e
        high(st, ("qkv", 0, 0), None, first=True)
        high(st, ("qkv", 0, 1), None, first=True)
        for g in range(3):
            d = DIL[g]
            if g:
                e.wait_ge(misc_ready, M("lT", g - 1).nth)
            for j in range(3):
                for t in range(2):
                    n = 2 * j + t
                    gr = G("qkv", g, n)
                    o = gr.take(e)
                    dst = (qT if n < 3 else kT)[:, n % 3, :]
                    st.w()
                    gr.done(st, e.activation(res(dst, d), perm(o[:, :], d), ACT.Copy))
                    st.w()
                    e.sem_inc(sem("qk_ready"), 1)
                high(st, ("qkv", g, j), G("qkv", g, 2 * j + 1))
            if g == 2:
                for m in range(3):
                    gr = G("qkv", g, 6 + m)
                    o = gr.take(e)
                    st.w()
                    gr.done(st, e.activation(res(vT[:, m, :], d), perm(o[:, :], d), ACT.Copy))
                st.w()
                e.sem_inc(sem("vT_ready"), 3)
            for t in range(NT):
                gr = G("qkv", g, 6 + t) if g < 2 else M("vt", t)
                o = gr.take(e)
                st.w()
                gr.done(st, e.activation(vt[:, t, :], o[:, 0:GW], ACT.Copy))
                st.w()
                e.sem_inc(sem("v_ready"), 1)
            last = G("qkv", g, 9 if g < 2 else 8)
            high(st, ("qkv", g, 3), last)
            high(st, ("qkv", g, 4), last)
            for h in range(HG):
                u = 6 * g + h
                w = 256 if g == 0 else P
                e.wait_ge(sem("max_ready"), u + 1)
                st.w()
                for n in range(4):
                    x = sc[:, u % 2, n * w + (P if g == 0 and n == 0 else 0):(n + 1) * w]
                    st.s(e.activation(x, x, ACT.Exp, bias=stat[:, 1, n, h:h + 1], accum_out=stat[:, 2, n, h:h + 1]))
                st.w()
                e.sem_inc(sem("prob_ready"), 1)
                nb = len(KEYS[g])
                for b in range((nb + 3) // 4):
                    gr = M("t", g, h, b)
                    o = gr.take(e)
                    n = min(4, nb - 4 * b) * P
                    if u >= 2 and b == 0:
                        e.wait_ge(misc_ready, M("o", (u - 2) // 6, (u - 2) % 6).nth)
                    gr.done(st, e.activation(pT[:, u % 2, 4 * b * P:4 * b * P + n], o[:, 0:n], ACT.Copy))
                st.w()
                e.sem_inc(sem("pT_ready"), 1)
            st.s(e.activation(stat[:, 5, :, :], stat[:, 2, :, :], ACT.Ln))
            st.w()
            e.sem_inc(sem("ln_ready"), 1)
        for g in range(3):
            e.wait_ge(sem("lmax_ready"), g + 1)
            st.f(e.activation(lT[:, g, :], lT[:, g, :], ACT.Exp), sem("lexp_ready"), g + 1)
        split_act(st, lambda k: mg[:, k, :], 3, 0, lambda e, k: e.wait_ge(sem("comb_ready"), k + 1))

    def attn_dve(st):
        e = st.e
        low(st, ("qkv", 0, 0), first=True)
        low(st, ("qkv", 0, 1), first=True)
        for b in range(2):
            st.s(e.memset(sc[:, b, 0:P], NEG))
        for g in range(3):
            d = DIL[g]
            for j in range(5):
                low(st, ("qkv", g, j))
            e.wait_ge(sem("bias_in"), 96 * (g + 1))
            if g == 0:
                e.wait_ge(sem("msk_in"), 32)
            if g == 2:
                for h in range(HG):
                    st.s(e.tensor_tensor(biasT[:, h, P:256], biasT[:, h, P:256], msk[:, 0:P], ALU.add))

            def front(h):
                u = 6 * g + h
                if u >= 2:
                    hh = (u - 2) % 6
                    e.wait_ge(misc_ready, M("t", (u - 2) // 6, hh, 1 if (u - 2) // 6 == 0 else 0).nth)
                    e.wait_ge(sem("pT_ready"), u - 1)
                st.w()
                if g == 0:
                    gr = M("s", g, h, 0)
                    o = gr.take(e)
                    st.s(e.scalar_tensor_tensor(out=sc[:, u % 2, P:256], in0=o[:, P:256], scalar=0.125,
                                                in1=biasT[:, h, P:256], op0=ALU.mult, op1=ALU.add))
                    gr.done(st, e.scalar_tensor_tensor(out=sc[:, u % 2, 256:512], in0=o[:, 256:512], scalar=0.125,
                                                       in1=biasT[:, h, :], op0=ALU.mult, op1=ALU.add))
                    gr = M("s", g, h, 1)
                    o = gr.take(e)
                    gr.done(st, e.scalar_tensor_tensor(
                        out=sc[:, u % 2, 512:1024].rearrange("p (n k) -> p n k", n=2),
                        in0=o[:, :].rearrange("p (n k) -> p n k", n=2), scalar=0.125,
                        in1=biasT[:, h:h + 1, :].broadcast_to([P, 2, 256]), op0=ALU.mult, op1=ALU.add))
                    view = sc[:, u % 2, :].rearrange("p (n k) -> p n k", n=4)
                else:
                    gr = M("s", g, h, 0)
                    o = gr.take(e)
                    view = sc[:, u % 2, 0:512].rearrange("p (n k) -> p n k", n=4)
                    gr.done(st, e.scalar_tensor_tensor(
                        out=view, in0=o[:, :].rearrange("p (n k) -> p n k", n=4), scalar=0.125,
                        in1=biasT[:, h:h + 1, P:256].broadcast_to([P, 4, P]), op0=ALU.mult, op1=ALU.add))
                st.w()
                st.s(e.tensor_reduce(stat[:, 0, :, h], view, AX, ALU.max))
                st.w()
                st.s(e.tensor_scalar(stat[:, 1, :, h], stat[:, 0, :, h], -1.0, None, ALU.mult))
                st.w()
                e.sem_inc(sem("max_ready"), 1)

            def back(h):
                u = 6 * g + h
                e.wait_ge(sem("prob_ready"), u + 1)
                st.s(e.reciprocal(stat[:, 3, :, h], stat[:, 2, :, h]))
                gr = M("o", g, h)
                o = gr.take(e)
                if h == 0 and g:
                    e.wait_ge(misc_ready, M("oT", g - 1, 2).nth)
                st.w()
                gr.done(st, e.tensor_tensor(otok[:, :, h * HD:(h + 1) * HD],
                                            o[:, 0:4 * HD].rearrange("p (n d) -> p n d", n=4),
                                            stat[:, 3, :, h:h + 1].broadcast_to([P, 4, HD]), ALU.mult))
                st.w()
                e.sem_inc(sem("otok_ready"), 1)

            for h in range(HG + 1):
                if h < HG:
                    front(h)
                if h > 0:
                    back(h - 1)
            e.sem_inc(sem("bias_used"), 1)
            e.wait_ge(sem("ln_ready"), g + 1)
            st.s(e.tensor_tensor(stat[:, 4, :, :], stat[:, 5, :, :], stat[:, 0, :, :], ALU.add))
            st.w()
            e.sem_inc(sem("lse_ready"), 1)
            for m in range(3):
                gr = M("oT", g, m)
                o = gr.take(e)
                gr.done(st, e.tensor_copy(perm(group_out(g, m), d), res(o[:, :], d)))
            gr = M("lT", g)
            o = gr.take(e)
            gr.done(st, e.tensor_copy(perm(lT[:, g, :], d), res(o[0:HG, :], d)))
            st.w()
        st.s(e.tensor_tensor(lx[:, 0, :], lT[:, 0, :], lT[:, 1, :], ALU.max))
        st.w()
        st.s(e.tensor_tensor(lx[:, 0, :], lx[:, 0, :], lT[:, 2, :], ALU.max))
        st.w()
        for g in range(3):
            st.s(e.tensor_tensor(lT[:, g, :], lT[:, g, :], lx[:, 0, :], ALU.subtract))
            st.w()
            e.sem_inc(sem("lmax_ready"), 1)
        e.wait_ge(sem("lexp_ready"), 3)
        st.s(e.tensor_tensor(lx[:, 1, :], lT[:, 0, :], lT[:, 1, :], ALU.add))
        st.w()
        st.s(e.tensor_tensor(lx[:, 1, :], lx[:, 1, :], lT[:, 2, :], ALU.add))
        st.w()
        st.s(e.reciprocal(lx[:, 1, :], lx[:, 1, :]))
        st.w()
        for g in range(3):
            st.s(e.tensor_tensor(lT[:, g, :], lT[:, g, :], lx[:, 1, :], ALU.mult))
        st.w()
        e.sem_inc(sem("alpha_ready"), 1)
        for m in range(3):
            for g in range(3):
                gr = M("al", m, g)
                o = gr.take(e)
                gr.done(st, e.tensor_tensor(group_out(g, m), group_out(g, m), o[:, :], ALU.mult))
            st.w()
            for g in (1, 2):
                st.s(e.tensor_tensor(mg[:, m, :], mg[:, m, :], group_out(g, m), ALU.add))
                st.w()
            e.sem_inc(sem("comb_ready"), 1)
        split_dve(st, lambda k: mg[:, k, :], 3, 0)

    pw = Work(WK, WEND)
    dH = pw.get("dH", [P, KD, S], F32R)
    dL = pw.get("dL", [P, KD, S], F32R)
    PAD = 16
    win = pw.get("win", [P, 3, PAD + S])
    dif = pw.get("dif", [P, 2, S])

    def pool_sp(e):
        with e.Fori(0, 2) as i:
            for j in range(2):
                load(e, ("pin", j), by_k(w1, KD, 2 * P, POOL0 + i * 4 * P + j * 2 * P), None, i, 2)

        def parts(slot):
            d = slot[:, 0:CH].rearrange("p (g k n) -> p g k n", g=4, k=2)
            s = a["pool_w"][0].rearrange("g (k p) n -> p g k n", p=P)
            return [(d[:, :, k, :], s[:, :, k, :]) for k in range(2)]
        load(e, ("pw",), parts)

    def pool_pe(pe):
        with pe.Fori(0, 2) as i:
            for j in range(2):
                slot = use(pe, ("pin", j), None, i, 2)
                for t in range(2):
                    g = G("pin", j, t, i=i, n=4)
                    o = g.open(pe)
                    g.close(product(pe, o[:, :], slot, KD, 2 * P, t * P, P, uH, uL))
        slot = use(pe, ("pw",))
        for m in range(KD):
            g = G("pw", m)
            o = g.open(pe)
            x = 2 * (m // 2)
            pe.wait_ge(sem("d_ready"), x + 2)
            g.close(product(pe, o[:, :], slot, 2, 2 * P, (m % 2) * P, P, dH[:, x:x + 2, :], dL[:, x:x + 2, :],
                            off=(m // 2) * 4 * P))

    def pool_act(st):
        e = st.e
        for j in range(4):
            for t in range(2):
                m = 2 * j + t
                g = G("pin", j, t)
                o = g.take(e)
                if m:
                    e.wait_ge(sem("win_free"), m)
                st.w()
                g.done(st, e.activation(win[:, 0, PAD:], o[:, :], ACT.Copy))
                st.w()
                e.sem_inc(sem("win_ready"), 1)
                e.wait_ge(sem("dif_ready"), m + 1)
                st.f(e.activation(dH[:, m, :], dif[:, m % 2, :], ACT.Copy), sem("dH_ready"), m + 1)
            high(st, ("pin", j), G("pin", j, 1))
        for m in range(KD):
            g = G("pw", m)
            o = g.take(e)
            st.w()
            st.f(e.activation(bH[:, m, :], o[:, :], ACT.Copy, scale=PT[:, 0, 32 + m:33 + m]), sem("bH_ready"), 3 + m + 1)
        high(st, ("pw",), G("pw", KD - 1))

    def pool_dve(st):
        e = st.e
        st.s(e.memset(win[:, :, 0:PAD], 0.0))
        st.w()
        for j in range(4):
            w = POOLW[j]
            for t in range(2):
                m = 2 * j + t
                e.wait_ge(sem("win_ready"), m + 1)
                src, step = 0, 1
                while step < w:
                    dst = 1 if src != 1 else 2
                    st.s(e.tensor_tensor(win[:, dst, PAD:], win[:, src, PAD:], win[:, src, PAD - step:PAD - step + S], ALU.add))
                    st.w()
                    src, step = dst, 2 * step
                st.s(e.tensor_tensor(win[:, src, PAD:2 * PAD], win[:, src, PAD:2 * PAD], C("edge")[:, 16 * j:16 * j + 16], ALU.mult))
                st.w()
                if m >= 2:
                    e.wait_ge(sem("dH_ready"), m - 1)
                st.s(e.scalar_tensor_tensor(out=dif[:, m % 2, :], in0=win[:, src, PAD:], scalar=1.0 / w,
                                            in1=win[:, 0, PAD:], op0=ALU.mult, op1=ALU.subtract))
                st.w()
                e.sem_inc(sem("dif_ready"), 1)
                e.sem_inc(sem("win_free"), 1)
                e.wait_ge(sem("dH_ready"), m + 1)
                st.f(e.tensor_tensor(dL[:, m, :], dif[:, m % 2, :], dH[:, m, :].bitcast(F32), ALU.subtract), sem("d_ready"), m + 1)
            low(st, ("pin", j))
        for m in range(KD):
            g = G("pw", m)
            o = g.take(e)
            e.wait_ge(sem("bH_ready"), 3 + m + 1)
            st.w()
            st.s(e.tensor_scalar(dif[:, m % 2, :], o[:, :], PT[:, 0, 32 + m:33 + m], None, ALU.mult))
            st.w()
            g.done(st, e.tensor_tensor(bL[:, m, :], dif[:, m % 2, :], bH[:, m, :].bitcast(F32), ALU.subtract))
            st.w()
            e.sem_inc(sem("b_ready"), 1)
        low(st, ("pw",))

    zw = Work(WK, WEND)
    xc = zw.get("xc", [P, 12, S])
    cvt = zw.get("cvt", [P, 2, S])
    ta = zw.get("ta", [P, 2, S])
    dec = zw.get("dec", [P, 2, S])
    ytok = zw.get("ytok", [P, D])
    dts = zw.get("dts", [P, 6, 4, 16])
    avec = zw.get("avec", [P, 4, 16])
    dtb = zw.get("dtb", [P, 2, 16])
    ex = zw.get("ex", [P, 3, 16])
    xdt = at("xdt", [P, 4, D], F32, Z)
    yw = Work(Z + 16384, Z + 32768)
    btok = yw.get("btok", [P, 4, 256])
    prev = yw.get("prev", [P, D])
    xdd = yw.get("xdd", [P, S])
    cbm = yw.get("cbm", [P, 2, P])
    yoff = yw.get("yoff", [P, S])

    def ssd_sp(e):
        def parts(slot):
            d = slot[:, 0:KD * 16].rearrange("p (k n) -> p k n", k=KD)
            s = kcols(w1, 0, KD, DT0, 16)
            return [(d[:, 0:4, :], s[:, 0:4, :]), (d[:, 4:8, :], s[:, 4:8, :])]
        load(e, ("dt",), parts)
        with e.Fori(0, 3) as i:
            for j in range(2):
                load(e, ("xbc", j), by_k(w1, KD, 2 * P, XBC0 + i * 4 * P + j * 2 * P), None, i, 2)
        with e.Fori(0, 2) as i:
            for j in range(2):
                load(e, ("z", j), by_k(w1, KD, 2 * P, Z0 + i * 4 * P + j * 2 * P), None, i, 2)

    def ssd_pool(e):
        e.wait_ge(sem("b_ready"), 11)
        e.dma_start(dtb[:, 0, :], a["ssd_dt_bias"][0].partition_broadcast(P)).then_inc(sem("dtb_in"), 16)
        e.dma_start(dtb[:, 1, :], a["ssd_a_log"][0].partition_broadcast(P)).then_inc(sem("dtb_in"), 16)

    def ssd_pe(pe):
        slot = use(pe, ("dt",))
        g = G("dt")
        o = g.open(pe)
        for t in range(NT):
            ins = product_tok(pe, o[:, 16 * t:16 * t + 16], slot, KD, 16, 16,
                              lambda k: uH[:, k, t * P:(t + 1) * P], lambda k: uL[:, k, t * P:(t + 1) * P])
        g.close(ins)
        with pe.Fori(0, 3) as i:
            for j in range(2):
                slot = use(pe, ("xbc", j), None, i, 2)
                for t in range(2):
                    g = G("xbc", j, t, i=i, n=4)
                    o = g.open(pe)
                    g.close(product(pe, o[:, :], slot, KD, 2 * P, t * P, P, uH, uL))
        pe.wait_ge(sem("xc_ready"), 12)
        for x in range(2):
            g = M("bt", x)
            o = g.open(pe)
            for c in range(4):
                ins = pe.transpose(o[:, c * P:(c + 1) * P], xc[:, 8 + x, c * P:(c + 1) * P], C("ident"))
            g.close(ins)
        for c in range(4):
            for x in range(2):
                g = M("xt", c, x)
                o = g.open(pe)
                for m in range(4):
                    ins = pe.transpose(o[:, m * P:(m + 1) * P], xc[:, 4 * x + m, c * P:(c + 1) * P], C("ident"))
                g.close(ins)
        pe.wait_ge(sem("a_ready"), 1)
        for c in range(4):
            g = M("ac", c)
            o = g.open(pe)
            for x, name in enumerate(("gt", "le", "ones")):
                ins = pe.matmul(o[:, 16 * x:16 * x + 16], C(name), avec[:, c, :], start=True, stop=True)
            g.close(ins)
            g = M("cb", c)
            o = g.open(pe)
            for x in range(2):
                ins = pe.matmul(o[:, x * P:(x + 1) * P], xc[:, 8 + x, c * P:(c + 1) * P], xc[:, 10 + x, c * P:(c + 1) * P],
                                start=True, stop=True)
            g.close(ins)
            for q in range(4):
                n = 4 * c + q
                pe.wait_ge(sem("ta_ready"), n + 1)
                g = M("seg", c, q)
                o = g.open(pe)
                g.close(pe.matmul(o[:, :], C("gt"), ta[:, n % 2, :], start=True, stop=True))
                if q % 2 == 0:
                    continue
                x = q // 2
                g = M("yd", c, x)
                o = g.open(pe)
                for r in range(2):
                    pe.wait_ge(sem("m_ready"), n + r)
                    for h in range(4):
                        ins = pe.matmul(o[:, (4 * r + h) * HD:(4 * r + h + 1) * HD], dec[:, (n - 1 + r) % 2, h * P:(h + 1) * P],
                                        xdt[:, c, (8 * x + 4 * r + h) * HD:(8 * x + 4 * r + h + 1) * HD], start=True, stop=True)
                g.close(ins)
                if c > 0:
                    pe.wait_ge(sem("prev_ready"), 2 * c)
                    g = M("yo", c, x)
                    o = g.open(pe)
                    g.close(pe.matmul(o[:, :], xc[:, 10 + x, c * P:(c + 1) * P], prev[:, x * S:(x + 1) * S], start=True, stop=True))
                if c < 3:
                    pe.wait_ge(sem("xdd_ready"), 2 * c + x + 1)
                    g = M("st", c, x)
                    o = g.open(pe)
                    g.close(pe.matmul(o[:, :], btok[:, c, x * P:(x + 1) * P], xdd[:, :], start=True, stop=True))
            pe.wait_ge(sem("ytok_ready"), 2 * c + 2)
            for x in range(2):
                g = M("yT", c, x)
                o = g.open(pe)
                for m in range(4):
                    ins = pe.transpose(o[:, m * P:(m + 1) * P], ytok[:, (4 * x + m) * P:(4 * x + m + 1) * P], C("ident"))
                g.close(ins)
        with pe.Fori(0, 2) as i:
            for j in range(2):
                slot = use(pe, ("z", j), None, i, 2)
                for t in range(2):
                    g = G("z", j, t, i=i, n=4)
                    o = g.open(pe)
                    g.close(product(pe, o[:, :], slot, KD, 2 * P, t * P, P, uH, uL))
        for x in range(2):
            g = M("yn", x)
            o = g.open(pe)
            for m in range(4):
                pe.wait_ge(sem("ysq_ready"), 4 * x + m + 1)
                ins = pe.matmul(o[:, :], C("ones"), ysq[:, m, :], start=m == 0, stop=m == 3)
            g.close(ins)

    ysq = at("ysq", [P, 4, S], F32, WK + 12 * 2048)

    def ssd_act(st):
        e = st.e
        e.wait_ge(sem("dtb_in"), 32)
        e.wait_ge(sem("v_dt_ready"), 1)
        st.s(e.activation(dts[:, 1], dts[:, 1], ACT.Exp, scale=-1.0))
        st.s(e.activation(dtb[:, 1, :], dtb[:, 1, :], ACT.Exp))
        st.w()
        e.sem_inc(sem("edt_ready"), 1)
        e.wait_ge(sem("udt_ready"), 1)
        st.s(e.activation(dts[:, 4], dts[:, 2], ACT.Ln))
        st.w()
        e.sem_inc(sem("ldt_ready"), 1)
        high(st, ("dt",), G("dt"))
        for j in range(6):
            for t in range(2):
                m = 2 * j + t
                g = G("xbc", j, t)
                o = g.take(e)
                if m >= 2:
                    e.wait_ge(sem("xc_ready"), m - 1)
                st.w()
                st.s(e.activation(cvt[:, m % 2, :], o[:, :], ACT.Identity, bias=PT[:, 0, 88 + m:89 + m], scale=PT[:, 0, 76 + m:77 + m]))
                st.w()
                e.sem_inc(sem("cv0_ready"), 1)
                e.wait_ge(sem("cv_ready"), m + 1)
                st.f(e.activation(xc[:, m, :], cvt[:, m % 2, :], ACT.Sigmoid), sem("xs_ready"), m + 1)
            high(st, ("xbc", j), G("xbc", j, 1))
        for c in range(4):
            g = M("ac", c)
            o = g.take(e)
            if c:
                e.wait_ge(sem("ex_used"), c)
            st.w()
            g.done(st, e.activation(ex[:, :, :].rearrange("p a h -> p (a h)"), o[:, 0:48], ACT.Exp))
            st.w()
            e.sem_inc(sem("ex_ready"), 1)
            for q in range(4):
                n = 4 * c + q
                g = M("seg", c, q)
                o = g.take(e)
                if n >= 2:
                    k = n - 2
                    e.wait_ge(misc_ready, M("yd", k // 4, (k % 4) // 2).nth)
                st.w()
                g.done(st, e.activation(dec[:, n % 2, :], o[:, :], ACT.Exp))
                st.w()
                e.sem_inc(sem("dec_ready"), 1)
        for j in range(4):
            for t in range(2):
                m = 2 * j + t
                g = G("z", j, t)
                o = g.take(e)
                e.wait_ge(sem("z_used"), max(m - 1, 0))
                st.w()
                st.f(e.activation(sg[:, m % 2, :], o[:, :], ACT.Sigmoid), sem("zs_ready"), m + 1)
                e.wait_ge(sem("yz_ready"), m + 1)
                if m >= 4:
                    e.wait_ge(misc_ready, M("yn", 0).nth)
                st.w()
                st.f(e.activation(ysq[:, m % 4, :], xc[:, m, :], ACT.Square), sem("ysq_ready"), m + 1)
            high(st, ("z", j), G("z", j, 1))
            if j % 2 == 1:
                x = j // 2
                e.wait_ge(sem("ymean_ready"), x + 1)
                st.w()
                st.f(e.activation(nrmt[:, :], nrmt[:, :], ACT.Sqrt), sem("yroot_ready"), x + 1)
        split_act(st, lambda k: xc[:, k, :], 8, 11, lambda e, k: e.wait_ge(sem("yfin_ready"), k + 1))

    def ssd_dve(st):
        e = st.e
        g = G("dt")
        o = g.take(e)
        e.wait_ge(sem("dtb_in"), 32)
        st.w()
        v, av, u, um, ln, dt = (dts[:, x] for x in range(6))
        g.done(st, e.tensor_tensor(v, o[:, 0:64].rearrange("p (c h) -> p c h", c=4),
                                   dtb[:, 0:1, :].broadcast_to([P, 4, 16]), ALU.add))
        st.w()
        st.s(e.tensor_scalar(av, v, -1.0, None, ALU.mult))
        st.w()
        st.s(e.tensor_tensor(av, av, v, ALU.max))
        st.w()
        e.sem_inc(sem("v_dt_ready"), 1)
        e.wait_ge(sem("edt_ready"), 1)
        st.s(e.tensor_scalar(u, av, 1.0, None, ALU.add))
        st.w()
        e.sem_inc(sem("udt_ready"), 1)
        st.s(e.tensor_scalar(um, u, -1.0, None, ALU.add))
        st.w()
        st.s(e.tensor_scalar(dt, um, 0.0, None, ALU.is_equal))
        st.w()
        st.s(e.tensor_tensor(um, um, dt, ALU.add))
        st.w()
        st.s(e.reciprocal(um, um))
        e.wait_ge(sem("ldt_ready"), 1)
        st.s(e.tensor_tensor(ln, ln, dt, ALU.add))
        st.w()
        st.s(e.tensor_tensor(ln, ln, um, ALU.mult))
        st.w()
        st.s(e.tensor_tensor(ln, ln, av, ALU.mult))
        st.s(e.tensor_scalar(v, v, 0.0, None, ALU.max))
        st.w()
        st.s(e.tensor_tensor(dt, ln, v, ALU.add))
        st.s(e.tensor_scalar(dtb[:, 1, :], dtb[:, 1, :], -1.0, None, ALU.mult))
        st.w()
        st.s(e.tensor_tensor(avec[:, :, :], dt, dtb[:, 1:2, :].broadcast_to([P, 4, 16]), ALU.mult))
        st.w()
        e.sem_inc(sem("a_ready"), 1)
        low(st, ("dt",))
        for j in range(6):
            for t in range(2):
                m = 2 * j + t
                g = G("xbc", j, t)
                o = g.take(e)
                e.wait_ge(sem("cv0_ready"), m + 1)
                y = cvt[:, m % 2, :]
                for tap in (2, 1, 0):
                    back = 3 - tap
                    w = PT[:, 0, 40 + 12 * tap + m:41 + 12 * tap + m]
                    ins = e.scalar_tensor_tensor(out=y[:, back:], in0=o[:, 0:S - back], scalar=w, in1=y[:, back:],
                                                 op0=ALU.mult, op1=ALU.add)
                    if tap:
                        st.s(ins)
                    else:
                        g.done(st, ins)
                    st.w()
                e.sem_inc(sem("cv_ready"), 1)
                e.wait_ge(sem("xs_ready"), m + 1)
                st.s(e.tensor_tensor(xc[:, m, :], xc[:, m, :], y, ALU.mult))
                st.w()
                e.sem_inc(sem("xc_ready"), 1)
            low(st, ("xbc", j))
        for x in range(2):
            g = M("bt", x)
            o = g.take(e)
            g.done(st, e.tensor_copy(btok[:, :, x * P:(x + 1) * P], o[:, :].rearrange("p (c n) -> p c n", c=4)))
        for c in range(4):
            for x in range(2):
                g = M("xt", c, x)
                o = g.take(e)
                g.done(st, e.tensor_tensor(xdt[:, c, x * S:(x + 1) * S].rearrange("p (h d) -> p h d", h=8),
                                           o[:, :].rearrange("p (h d) -> p h d", h=8),
                                           dt[:, c, 8 * x:8 * x + 8].unsqueeze(2).broadcast_to([P, 8, HD]), ALU.mult))
        st.w()
        for m in range(8):
            st.s(e.tensor_scalar(xc[:, m, :], xc[:, m, :], PT[:, 3, 32 + m:33 + m], None, ALU.mult))
        st.w()

        def spread(n):
            c, q = n // 4, n % 4
            if n >= 2:
                e.wait_ge(misc_ready, M("seg", (n - 2) // 4, (n - 2) % 4).nth)
            st.w()
            st.s(e.tensor_tensor(ta[:, n % 2, :].rearrange("p (h t) -> p h t", h=4),
                                 C("le").unsqueeze(1).broadcast_to([P, 4, P]),
                                 avec[:, c, 4 * q:4 * q + 4].unsqueeze(2).broadcast_to([P, 4, P]), ALU.mult))
            st.w()
            e.sem_inc(sem("ta_ready"), 1)
        spread(0)
        for c in range(4):
            g = M("cb", c)
            o = g.take(e)
            st.w()
            g.done(st, e.tensor_tensor(cbm[:, :, :], o[:, 0:256].rearrange("p (g t) -> p g t", g=2),
                                       C("le").unsqueeze(1).broadcast_to([P, 2, P]), ALU.mult))
            e.wait_ge(sem("ex_ready"), c + 1)
            for q in range(4):
                n = 4 * c + q
                if n + 1 < 16:
                    spread(n + 1)
                e.wait_ge(sem("dec_ready"), n + 1)
                x = q // 2
                st.w()
                mm = dec[:, n % 2, :].rearrange("p (h t) -> p h t", h=4)
                st.s(e.tensor_tensor(mm, mm, cbm[:, x:x + 1, :].broadcast_to([P, 4, P]), ALU.mult))
                st.w()
                e.sem_inc(sem("m_ready"), 1)
                if q % 2 == 0:
                    continue
                if c < 3:
                    if 2 * c + x >= 1:
                        k = 2 * c + x - 1
                        e.wait_ge(misc_ready, M("st", k // 2, k % 2).nth)
                    st.s(e.tensor_tensor(xdd[:, :].rearrange("p (h d) -> p h d", h=8),
                                         xdt[:, c, x * S:(x + 1) * S].rearrange("p (h d) -> p h d", h=8),
                                         ex[:, 0, 8 * x:8 * x + 8].unsqueeze(2).broadcast_to([P, 8, HD]), ALU.mult))
                    st.w()
                    e.sem_inc(sem("xdd_ready"), 1)
                g = M("yd", c, x)
                o = g.take(e)
                if c:
                    e.wait_ge(misc_ready, M("yT", c - 1, 1).nth)
                y = ytok[:, x * S:(x + 1) * S]
                if c == 0:
                    g.done(st, e.tensor_copy(y, o[:, :]))
                else:
                    g2 = M("yo", c, x)
                    o2 = g2.take(e)
                    g2.done(st, e.tensor_tensor(yoff[:, :].rearrange("p (h d) -> p h d", h=8),
                                                o2[:, :].rearrange("p (h d) -> p h d", h=8),
                                                ex[:, 1, 8 * x:8 * x + 8].unsqueeze(2).broadcast_to([P, 8, HD]), ALU.mult))
                    st.w()
                    g.done(st, e.tensor_tensor(y, yoff[:, :], o[:, :], ALU.add))
                st.w()
                e.sem_inc(sem("ytok_ready"), 1)
                if c < 3:
                    g = M("st", c, x)
                    o = g.take(e)
                    pv = prev[:, x * S:(x + 1) * S]
                    if c == 0:
                        g.done(st, e.tensor_copy(pv, o[:, :]))
                    else:
                        st.s(e.tensor_tensor(pv.rearrange("p (h d) -> p h d", h=8), pv.rearrange("p (h d) -> p h d", h=8),
                                             ex[:, 2, 8 * x:8 * x + 8].unsqueeze(2).broadcast_to([P, 8, HD]), ALU.mult))
                        st.w()
                        g.done(st, e.tensor_tensor(pv, pv, o[:, :], ALU.add))
                    st.w()
                    e.sem_inc(sem("prev_ready"), 1)
            e.sem_inc(sem("ex_used"), 1)
            for x in range(2):
                g = M("yT", c, x)
                o = g.take(e)
                y = xc[:, 4 * x:4 * x + 4, c * P:(c + 1) * P]
                g.done(st, e.tensor_tensor(y, y, o[:, :].rearrange("p (m t) -> p m t", m=4), ALU.add))
        st.w()
        for j in range(4):
            for t in range(2):
                m = 2 * j + t
                g = G("z", j, t)
                o = g.take(e)
                e.wait_ge(sem("zs_ready"), m + 1)
                st.w()
                g.done(st, e.tensor_tensor(sg[:, m % 2, :], o[:, :], sg[:, m % 2, :], ALU.mult))
                st.w()
                st.s(e.tensor_tensor(xc[:, m, :], xc[:, m, :], sg[:, m % 2, :], ALU.mult))
                st.w()
                e.sem_inc(sem("yz_ready"), 1)
                e.sem_inc(sem("z_used"), 1)
            low(st, ("z", j))
            if j % 2 == 1:
                x = j // 2
                g = M("yn", x)
                o = g.take(e)
                st.w()
                g.done(st, e.tensor_scalar(nrmt[:, :], o[:, :], 1.0 / 512, EPS, ALU.mult, ALU.add))
                st.w()
                e.sem_inc(sem("ymean_ready"), 1)
                e.wait_ge(sem("yroot_ready"), x + 1)
                st.s(e.reciprocal(nrmt[:, :], nrmt[:, :]))
                st.w()
                for m in range(4 * x, 4 * x + 4):
                    st.s(e.scalar_tensor_tensor(out=xc[:, m, :], in0=xc[:, m, :], scalar=PT[:, 0, 100 + m:101 + m],
                                                in1=nrmt[:, :], op0=ALU.mult, op1=ALU.mult))
                st.w()
                e.sem_inc(sem("yfin_ready"), 4)
        split_dve(st, lambda k: xc[:, k, :], 8, 11)

    fw = Work(Z + 65536, WEND)
    cva = at("cva", [P, 2, S], F32, BASE + 49152)
    cvv = at("cvv", [P, 2, S], F32, BASE + 49152 + 4096)
    sga = at("sga", [P, 2, S], F32, BASE + 49152 + 8192)

    def ffn_sp(e):
        wu, wd = a["ffn_w_up"][0], a["ffn_w_down"][0]
        for r in range(2):
            c0 = r * FR * P
            with e.Fori(0, FR // 2) as i:
                for j in range(2):
                    load(e, ("up", r, j), by_cols(wu, KD, c0 + i * 2 * P + j * P, FF + c0 + i * 2 * P + j * P), None, i, 2)
            j = FR - 1
            load(e, ("up", r, j), by_cols(wu, KD, c0 + j * P, FF + c0 + j * P))
            with e.Fori(0, 2) as i:
                for j in range(4):
                    load(e, ("dn", r, j), by_k(wd, FR, P, i * 4 * P + j * P, c0), None, i, 4)

    def ffn_pe(pe):
        for r in range(2):
            def up(j, i, n):
                slot = use(pe, ("up", r, j), None, i, n)
                if r == 0 and j == 0:
                    product_pair(pe, [G("up", r, j, t, i=i, n=2 * n) for t in range(2)], slot, KD, uH, uL, u_tile(1))
                    return
                for t in range(2):
                    g = G("up", r, j, t, i=i, n=2 * n)
                    o = g.open(pe)
                    g.close(product(pe, o[:, :], slot, KD, 2 * P, t * P, P, uH, uL))
            with pe.Fori(0, FR // 2) as i:
                up(0, i, 2)
                up(1, i, 2)
            up(FR - 1, 0, 0)
            with pe.Fori(0, 2) as i:
                for j in range(4):
                    slot = use(pe, ("dn", r, j), None, i, 4)
                    g = G("dn", r, j, i=i, n=4)
                    o = g.open(pe)
                    ready = lambda k: (sem("mid_ready"), FR * r + k + 1)
                    g.close(product(pe, o[:, :], slot, FR, P, 0, P, mH, mL, tile_ready=ready if j == 0 else None))

    def ffn_act(st):
        e = st.e
        for r in range(2):
            if r:
                e.wait_ge(gemm_ready, G("dn", 0, KD - 1).nth)
            for j in range(FR):
                n = FR * r + j
                for t, cv in ((0, cva), (1, cvv)):
                    g = G("up", r, j, t)
                    o = g.take(e)
                    f = 22 * t + n
                    if n >= 2:
                        e.wait_ge(sem("mid_ready"), n - 1)
                    st.w()
                    st.s(e.activation(cv[:, n % 2, :], o[:, :], ACT.Identity, bias=PT[:, 2, 44 + f:45 + f], scale=PT[:, 2, f:f + 1]))
                    st.w()
                    e.sem_inc(sem("fcv0_ready"), 1)
                e.wait_ge(sem("fcva_ready"), n + 1)
                st.f(e.activation(sga[:, n % 2, :], cva[:, n % 2, :], ACT.Sigmoid), sem("fsg_ready"), n + 1)
                high(st, ("up", r, j), G("up", r, j, 1))
                e.wait_ge(sem("fh_ready"), n + 1)
                st.w()
                st.f(e.activation(mH[:, j, :], sga[:, n % 2, :], ACT.Copy), sem("midH_ready"), n + 1)
            for j in range(KD):
                high(st, ("dn", r, j), G("dn", r, j))

    def ffn_dve(st):
        e = st.e
        for r in range(2):
            for j in range(FR):
                n = FR * r + j
                for t, cv in ((0, cva), (1, cvv)):
                    g = G("up", r, j, t)
                    o = g.take(e)
                    f = 22 * t + n
                    e.wait_ge(sem("fcv0_ready"), 2 * n + t + 1)
                    y = cv[:, n % 2, :]
                    st.w()
                    st.s(e.scalar_tensor_tensor(out=y[:, 1:], in0=o[:, 0:S - 1], scalar=PT[:, 1, 44 + f:45 + f], in1=y[:, 1:],
                                                op0=ALU.mult, op1=ALU.add))
                    st.w()
                    g.done(st, e.scalar_tensor_tensor(out=y[:, 2:], in0=o[:, 0:S - 2], scalar=PT[:, 1, f:f + 1], in1=y[:, 2:],
                                                      op0=ALU.mult, op1=ALU.add))
                    if t == 0:
                        st.w()
                        e.sem_inc(sem("fcva_ready"), 1)
                e.wait_ge(sem("fsg_ready"), n + 1)
                st.w()
                h = sga[:, n % 2, :]
                st.s(e.tensor_tensor(h, h, cva[:, n % 2, :], ALU.mult))
                st.w()
                st.s(e.tensor_tensor(h, h, cvv[:, n % 2, :], ALU.mult))
                st.w()
                e.sem_inc(sem("fh_ready"), 1)
                low(st, ("up", r, j))
                e.wait_ge(sem("midH_ready"), n + 1)
                st.w()
                st.s(e.tensor_tensor(mL[:, j, :], h, mH[:, j, :].bitcast(F32), ALU.subtract))
                st.w()
                e.sem_inc(sem("mid_ready"), 1)
            for j in range(KD):
                g = G("dn", r, j)
                o = g.take(e)
                st.w()
                g.done(st, e.tensor_tensor(hT[:, j, :], hT[:, j, :], o[:, :], ALU.add))
                if r == 1:
                    st.w()
                    e.sem_inc(sem("h_ready"), 1)
                low(st, ("dn", r, j))

    XB = {"d": ("dq", "dk"), "r": ("rq", "rk"), "g": ("gq", "gk")}
    ROT = {"d": "rot_d", "r": "rot_r", "g": "rot_g"}
    ROPE = {"d": 0, "r": 1, "g": 2}
    TILES = {"d": 8, "r": 8, "g": 6}

    bw = Work(WK, WEND)
    qk = bw.get("qk", [P, 8, S])
    vv = bw.get("vv", [P, NT, S])
    cs = bw.get("cs", [P, 2 * S])
    rest = bw.o
    rw = Work(rest, WEND)
    raw = rw.get("raw", [P, 2, S])
    sq = rw.get("sq", [P, 2, S])
    rs = rw.get("rs", [P, 2, S])
    xn = rw.get("xn", [P, 2, S])

    def rope_base(kind, l):
        return {"d": 0, "r": 8, "g": 16}[kind] + 22 * l, {"d": 0, "r": 0, "g": 8}[kind] + 14 * l

    def rope_sp(e, kind, l):
        if kind == "g":
            for j in range(2):
                load(e, (kind, j), by_k(w2[l], KD, 2 * P, COL2["gq"] + j * 2 * P), l)

            slot, used, nth = chunk((kind, 2), l, 0, 0)
            e.wait_ge(lo_ready, nth - 2)
            e.sem_inc(sem("slot_turns"), 1)
            d = wR[:, slot, 0:KD * 256].rearrange("p (k n) -> p k n", k=KD)
            for h in range(2):
                for twice, signal in ((0, sem("gk_in")), (1, raw_ready[slot])):
                    c = h * P + twice * HD
                    e.dma_start(d[:, :, c:c + HD], kcols(w2[l], 0, KD, COL2["gk"] + h * HD, HD)).then_inc(signal, 16)
        else:
            for j in range(4):
                load(e, (kind, j), by_k(w2[l], KD, 2 * P, COL2[XB[kind][0]] + j * 2 * P), l)

    def v_sp(e, kind, n, l):
        for j in range(n):
            cols = 2 * P if kind != "gv" else P
            load(e, (kind, j), by_k(w2[l], KD, cols, COL2[kind] + j * 2 * P), l)

    def v_pe(pe, kind, n, l):
        cols = 2 * P if kind != "gv" else P
        for j in range(n):
            slot = use(pe, (kind, j), l)
            if kind == "dv" and j == 0:
                product_tok_all(pe, [G(kind, j, t, l=l) for t in range(NT)], slot, cols, cols, u_tile(0, l))
                continue
            for t in range(NT):
                g = G(kind, j, t, l=l)
                o = g.open(pe)
                g.close(product_tok(pe, o[:, 0:cols], slot, KD, cols, cols,
                                    lambda k: uH[:, k, t * P:(t + 1) * P], lambda k: uL[:, k, t * P:(t + 1) * P]))

    VBASE = {"dv": 0, "rv": 8, "gv": 16}

    def v_act(st, kind, n, l):
        cols = 2 * P if kind != "gv" else P
        for j in range(n):
            for t in range(NT):
                g = G(kind, j, t, l=l)
                o = g.take(st.e)
                st.w()
                g.done(st, st.e.activation(vv[:, t, j * 2 * P:j * 2 * P + cols], o[:, 0:cols], ACT.Copy))
                st.w()
                st.e.sem_inc(sem("vv_ready"), 1)
            high(st, (kind, j), G(kind, j, NT - 1, l=l), l)

    def v_count(kind, l):
        return {"dv": 8, "rv": 16, "gv": 20}[kind] + 20 * l

    def v_dve(st, kind, n, l):
        for j in range(n):
            low(st, (kind, j), l)

    def rope_pe(pe, kind, l):
        n, norm = TILES[kind], kind != "r"
        b, bn = rope_base(kind, l)
        for t in range(n + 1):
            if t < n:
                if t % 2 == 0:
                    slot = use(pe, (kind, t // 2), l)
                g = G(kind, t, l=l)
                o = g.open(pe)
                g.close(product(pe, o[:, :], slot, KD, 2 * P, (t % 2) * P, P, uH, uL))
            if t > 0:
                pe.wait_ge(sem("raw_tile"), b + t)
                if norm:
                    g = M("ss", kind, t - 1, l=l)
                    o = g.open(pe)
                    g.close(pe.matmul(o[:, :], C("blk64"), sq[:, (t - 1) % 2, :], start=True, stop=True))
                g = M("rot", kind, t - 1, l=l)
                o = g.open(pe)
                g.close(pe.matmul(o[:, :], C(ROT[kind]), raw[:, (t - 1) % 2, :], start=True, stop=True))

    def rope_act(st, kind, l):
        e = st.e
        n, norm = TILES[kind], kind != "r"
        b, bn = rope_base(kind, l)

        def root(t):
            g = M("ss", kind, t, l=l)
            o = g.take(e)
            st.w()
            g.done(st, e.activation(rs[:, t % 2, :], o[:, :], ACT.Sqrt, bias=C("eps")[:, 0:1], scale=1.0 / HD))
            st.w()
            e.sem_inc(sem("rroot_ready"), 1)
        for t in range(n):
            g = G(kind, t, l=l)
            o = g.take(e)
            if kind != "d" or t >= 2:
                e.wait_ge(sem("rope_done"), b + max(t - 1, 0))
            st.w()
            if norm:
                c = {"d": 16, "g": 18}[kind] + (0 if t < 4 else 1)
                st.s(e.activation(raw[:, t % 2, :], o[:, :], ACT.Copy, scale=lp[:, c:c + 1]))
                g.done(st, e.activation(sq[:, t % 2, :], o[:, :], ACT.Square))
            else:
                g.done(st, e.activation(raw[:, t % 2, :], o[:, :], ACT.Copy))
            st.w()
            e.sem_inc(sem("raw_tile"), 1)
            if kind == "g" and t == 1:
                e.wait_ge(sem("gk_in"), 32 * l + 32)
            if t % 2 == 1:
                high(st, (kind, t // 2), g, l)
            if norm and t > 0:
                root(t - 1)
        if norm:
            root(n - 1)

    def rope_dve(st, kind, l):
        e = st.e
        n, norm = TILES[kind], kind != "r"
        b, bn = rope_base(kind, l)
        for t in range(n):
            x = raw[:, t % 2, :]
            e.wait_ge(sem("raw_tile"), b + t + 1)
            if t == 0:
                e.wait_ge(sem("cs_in"), 16 * ROPE[kind] + 16 + 48 * l)
                if kind == "g":
                    e.wait_ge(sem("b_ready"), 27 + 20 * l + 8)
                st.w()
            st.s(e.tensor_tensor(qk[:, t, :], x, cs[:, 0:S], ALU.mult))
            if t % 2 == 1:
                low(st, (kind, t // 2), l)
            g = M("rot", kind, t, l=l)
            o = g.take(e)
            st.w()
            g.done(st, e.tensor_tensor(xn[:, t % 2, :], o[:, :], cs[:, S:2 * S], ALU.mult))
            if norm:
                e.wait_ge(sem("rroot_ready"), bn + t + 1)
                st.s(e.reciprocal(rs[:, t % 2, :], rs[:, t % 2, :]))
            st.w()
            st.s(e.tensor_tensor(qk[:, t, :], qk[:, t, :], xn[:, t % 2, :], ALU.add))
            if norm:
                st.w()
                st.s(e.tensor_tensor(qk[:, t, :], qk[:, t, :], rs[:, t % 2, :], ALU.mult))
            st.w()
            e.sem_inc(sem("rope_done"), 1)

    def rope_pool(e, kind, l):
        c = {"d": lambda: (sem("h_ready"), 24 + 16 * l + 8), "r": lambda: (sem("b_ready"), 27 + 20 * l + 4),
             "g": lambda: (sem("b_ready"), 27 + 20 * l + 8)}[kind]()
        e.wait_ge(*c)
        e.sem_inc(sem("table_turns"), 1)
        e.dma_start(cs[:, :], ropes[ROPE[kind]]).then_inc(sem("cs_in"), 16)

    dw = Work(rest, WEND)
    wT = dw.get("wT", [P, 2, NT, S])
    ao = dw.get("ao", [P, 2, S])
    ast = dw.get("ast", [P, 3, 8])
    prA = at("prA", [P, 4, S], F32, Z + 8192)
    prB = at("prB", [P, 2, S], F32, Z + 16384 + 8192)
    rstd = nrmt

    def pr(i):
        return prA[:, i, :] if i < 4 else prB[:, i - 4, :]

    def turn_pe(pe, name, v, src, ready, l):
        pe.wait_ge(*ready)
        g = M(name, v, l=l)
        o = g.open(pe)
        for k in range(4):
            ins = pe.transpose(o[:, k * P:(k + 1) * P], src[:, k * P:(k + 1) * P], C("ident"))
        g.close(ins)

    def turn_act(st, name, pv, v, l):
        e = st.e
        g = M(name, v, l=l)
        o = g.take(e)
        h, n = v // 4, v % 4
        if n == 0 and h >= 2:
            e.wait_ge(misc_ready, M(pv, h - 2, l=l).nth)
        st.w()
        g.done(st, e.activation(wT[:, h % 2, :, n * P:(n + 1) * P], o[:, :].rearrange("p (k q) -> p k q", k=4), ACT.Copy))
        st.w()
        e.sem_inc(sem(name + "_turned"), 1)

    def diff_pe(pe, l):
        b, _ = rope_base("d", l)
        for u in range(20):
            if u < 16:
                h, n = u // 4, u % 4
                if n == 0:
                    pe.wait_ge(sem("rope_done"), b + 5 + h)
                for m in range(2):
                    g = G("s", u, m, l=l)
                    o = g.open(pe)
                    g.close(pe.matmul(o[:, :], qk[HD * m:HD * m + HD, h, n * P:(n + 1) * P],
                                      qk[HD * m:HD * m + HD, 4 + h, :], start=True, stop=True))
            if 2 <= u < 18:
                v = u - 2
                turn_pe(pe, "t", v, pr(2 * (v % 3)), (sem("dw_ready"), 16 * l + v + 1), l)
            if u >= 6 and u % 4 == 2:
                h = u // 4 - 1
                pe.wait_ge(sem("t_turned"), 16 * l + 4 * h + 4)
                if h == 0:
                    pe.wait_ge(sem("vv_ready"), v_count("dv", l))
                g = M("pv", h, l=l)
                o = g.open(pe)
                for k in range(NT):
                    ins = pe.matmul(o[:, :], vv[:, k, h * P:(h + 1) * P], wT[:, h % 2, k, :], start=k == 0, stop=k == NT - 1)
                g.close(ins)
            if u >= 7 and u % 4 == 3:
                h = u // 4 - 1
                pe.wait_ge(sem("aosq_ready"), 4 * l + h + 1)
                g = M("on", h, l=l)
                o = g.open(pe)
                g.close(pe.matmul(o[:, :], C("ones"), ao[:, 1, :], start=True, stop=True))

    def diff_act(st, l):
        e = st.e
        for u in range(21):
            if u < 16:
                e.wait_ge(sem("dmax_ready"), 16 * l + u + 1)
                if u >= 3:
                    e.wait_ge(misc_ready, M("t", u - 3, l=l).nth)
                st.w()
                for m in range(2):
                    g = G("s", u, m, l=l)
                    g.done(st, e.activation(pr(2 * (u % 3) + m), g.ps[:, :], ACT.Exp, bias=ast[:, u % 3, m:m + 1],
                                            scale=0.125, accum_out=ast[:, u % 3, 2 + m:3 + m]))
                st.w()
                e.sem_inc(sem("dexp_ready"), 1)
            if 2 <= u < 18:
                turn_act(st, "t", "pv", u - 2, l)
            if u >= 6 and u % 4 == 2:
                h = u // 4 - 1
                g = M("pv", h, l=l)
                o = g.take(e)
                if h:
                    e.wait_ge(sem("b_ready"), 27 + 20 * l + h)
                st.w()
                st.s(e.activation(ao[:, 0, :], o[:, :], ACT.Copy))
                g.done(st, e.activation(ao[:, 1, :], o[:, :], ACT.Square))
                st.w()
                e.sem_inc(sem("aosq_ready"), 1)
            if u >= 7 and u % 4 == 3:
                h = u // 4 - 1
                g = M("on", h, l=l)
                o = g.take(e)
                st.w()
                g.done(st, e.activation(rstd[:, :], o[:, :], ACT.Sqrt, bias=C("eps")[:, 1:2], scale=1.0 / P))
                st.w()
                e.sem_inc(sem("aoroot_ready"), 1)
            if u >= 8 and u % 4 == 0:
                h = u // 4 - 2
                e.wait_ge(sem("aofin_ready"), 4 * l + h + 1)
                st.w()
                st.f(e.activation(bH[:, h, :], ao[:, 0, :], ACT.Copy), sem("bH_ready"), 27 + 20 * l + h + 1)

    def diff_dve(st, l):
        e = st.e

        def front(u):
            if u >= 3:
                e.wait_ge(sem("dexp_ready"), 16 * l + u - 2)
            for m in range(2):
                g = G("s", u, m, l=l)
                o = g.take(e)
                st.w()
                st.s(e.tensor_reduce(ast[:, u % 3, m:m + 1], o[:, :], AX, ALU.max))
            st.w()
            st.s(e.tensor_scalar(ast[:, u % 3, 0:2], ast[:, u % 3, 0:2], -0.125, None, ALU.mult))
            st.w()
            e.sem_inc(sem("dmax_ready"), 1)

        def back(u):
            e.wait_ge(sem("dexp_ready"), 16 * l + u + 1)
            r = ast[:, u % 3, :]
            st.s(e.reciprocal(r[:, 4:6], r[:, 2:4]))
            st.w()
            st.s(e.tensor_tensor(r[:, 6:7], r[:, 5:6], lp[:, 25:26], ALU.mult))
            st.w()
            p0, p1 = pr(2 * (u % 3)), pr(2 * (u % 3) + 1)
            st.s(e.tensor_scalar(p1, p1, r[:, 6:7], None, ALU.mult))
            st.w()
            st.s(e.scalar_tensor_tensor(out=p0, in0=p0, scalar=r[:, 4:5], in1=p1, op0=ALU.mult, op1=ALU.add))
            st.w()
            e.sem_inc(sem("dw_ready"), 1)

        for u in range(21):
            if u < 16:
                front(u)
            if 1 <= u < 17:
                back(u - 1)
            if u >= 7 and u % 4 == 3:
                h = u // 4 - 1
                e.wait_ge(sem("aoroot_ready"), 4 * l + h + 1)
                st.w()
                st.s(e.reciprocal(rstd[:, :], rstd[:, :]))
                st.w()
                st.s(e.scalar_tensor_tensor(out=ao[:, 0, :], in0=ao[:, 0, :], scalar=lp[:, 20:21], in1=rstd[:, :],
                                            op0=ALU.mult, op1=ALU.mult))
                st.w()
                e.sem_inc(sem("aofin_ready"), 1)
            if u >= 8 and u % 4 == 0:
                h = u // 4 - 2
                e.wait_ge(sem("bH_ready"), 27 + 20 * l + h + 1)
                st.s(e.tensor_tensor(bL[:, h, :], ao[:, 0, :], bH[:, h, :].bitcast(F32), ALU.subtract))
                st.w()
                e.sem_inc(sem("b_ready"), 1)

    def gqa_pe(pe, l):
        b, _ = rope_base("g", l)
        pe.wait_ge(sem("rope_done"), b + 6)
        for u in range(35):
            if u < 32:
                h, n = u // 4, u % 4
                hp = HD * (h % 2)
                g = G("gs", u, l=l)
                o = g.open(pe)
                g.close(pe.matmul(o[:, :], qk[hp:hp + HD, h // 2, n * P:(n + 1) * P], qk[hp:hp + HD, 4 + h // 4, :],
                                  start=True, stop=True))
            if 2 <= u < 34:
                v = u - 2
                turn_pe(pe, "gt", v, pr(v % 4), (sem("gw_ready"), 32 * l + v + 1), l)
            if u >= 6 and u % 4 == 2:
                h = u // 4 - 1
                pe.wait_ge(sem("gt_turned"), 32 * l + 4 * h + 4)
                if h == 0:
                    pe.wait_ge(sem("vv_ready"), v_count("gv", l))
                g = M("gpv", h, l=l)
                o = g.open(pe)
                for k in range(NT):
                    ins = pe.matmul(o[0:HD, :], vv[:, k, (h // 4) * HD:(h // 4 + 1) * HD], wT[:, h % 2, k, :],
                                    start=k == 0, stop=k == NT - 1)
                g.close(ins)

    def gqa_act(st, l):
        e = st.e
        for u in range(35):
            if u < 32:
                e.wait_ge(sem("gmax_ready"), 32 * l + u + 1)
                if u >= 4:
                    e.wait_ge(misc_ready, M("gt", u - 4, l=l).nth)
                st.w()
                g = G("gs", u, l=l)
                g.done(st, e.activation(pr(u % 4), g.ps[:, :], ACT.Exp, bias=ast[:, u % 3, 0:1], scale=0.125,
                                        accum_out=ast[:, u % 3, 1:2]))
                st.w()
                e.sem_inc(sem("gexp_ready"), 1)
            if 2 <= u < 34:
                turn_act(st, "gt", "gpv", u - 2, l)
            if u >= 6 and u % 4 == 2:
                h = u // 4 - 1
                g = M("gpv", h, l=l)
                o = g.take(e)
                hp = HD * (h % 2)
                if h >= 2:
                    e.wait_ge(sem("b_ready"), 27 + 20 * l + 8 + h // 2)
                st.w()
                g.done(st, e.activation(ao[hp:hp + HD, 0, :], o[0:HD, :], ACT.Copy))
                if h % 2:
                    st.w()
                    st.f(e.activation(bH[:, h // 2, :], ao[:, 0, :], ACT.Copy), sem("bH_ready"), 27 + 20 * l + 8 + h // 2 + 1)

    def gqa_dve(st, l):
        e = st.e

        def split(h):
            e.wait_ge(sem("bH_ready"), 27 + 20 * l + 8 + h // 2 + 1)
            st.w()
            st.s(e.tensor_tensor(bL[:, h // 2, :], ao[:, 0, :], bH[:, h // 2, :].bitcast(F32), ALU.subtract))
            st.w()
            e.sem_inc(sem("b_ready"), 1)

        for u in range(33):
            if u < 32:
                g = G("gs", u, l=l)
                o = g.take(e)
                if u >= 3:
                    e.wait_ge(sem("gexp_ready"), 32 * l + u - 2)
                st.w()
                st.s(e.tensor_reduce(ast[:, u % 3, 0:1], o[:, :], AX, ALU.max))
                st.w()
                st.s(e.tensor_scalar(ast[:, u % 3, 0:1], ast[:, u % 3, 0:1], -0.125, None, ALU.mult))
                st.w()
                e.sem_inc(sem("gmax_ready"), 1)
            if u > 0:
                v = u - 1
                e.wait_ge(sem("gexp_ready"), 32 * l + v + 1)
                st.w()
                st.s(e.reciprocal(ast[:, v % 3, 2:3], ast[:, v % 3, 1:2]))
                st.w()
                st.s(e.tensor_scalar(pr(v % 4), pr(v % 4), ast[:, v % 3, 2:3], None, ALU.mult))
                st.w()
                e.sem_inc(sem("gw_ready"), 1)
            if u >= 11 and u % 8 == 3:
                split((u - 4) // 8 * 2 + 1)
        split(7)

    tw = Work(rest, WEND)
    rg = tw.get("rg", [P, 4, S])
    dst = tw.get("dst", [P, 2, DSTW])
    ro = tw.get("ro", [P, 2, S])
    dcy = at("dcy", [P, 2, DSTW], F32, Z + 8192)
    rsc = at("rsc", [P, 4, S], F32, Z + 16384 + 8192)
    rsq = nrmt

    def ret_pool(e, l):
        e.wait_ge(sem("b_ready"), 27 + 20 * l + 4)
        e.wait_ge(sem("rope_done"), 16 + 22 * l)
        e.sem_inc(sem("table_turns"), 1)
        e.dma_start(dst[:, :, :], dists.rearrange("p (a b) -> p a b", a=2)).then_inc(sem("dst_in"), 16)

    def ret_sp(e, l):
        for j in range(2):
            load(e, ("rg", j), by_k(w2[l], KD, 2 * P, COL2["rg"] + j * 2 * P), l)

    def ret_pe(pe, l):
        for j in range(2):
            slot = use(pe, ("rg", j), l)
            for t in range(2):
                g = G("rg", j, t, l=l)
                o = g.open(pe)
                g.close(product(pe, o[:, :], slot, KD, 2 * P, t * P, P, uH, uL))
        b, _ = rope_base("r", l)
        pe.wait_ge(sem("rope_done"), b + 8)
        pe.wait_ge(sem("vv_ready"), v_count("rv", l))
        for h in range(5):
            if h < 4:
                for j in range(4):
                    g = G("rs", h, j, l=l)
                    o = g.open(pe)
                    g.close(pe.matmul(o[:, :], qk[:, 4 + h, j * P:(j + 1) * P], qk[:, h, :], start=True, stop=True))
            if h > 0:
                pe.wait_ge(sem("ro_ready"), 4 * l + h)
                g = M("rm", h - 1, l=l)
                o = g.open(pe)
                g.close(pe.matmul(o[:, :], C("ones"), ro[:, (h - 1) % 2, :], start=True, stop=True))
            if h < 4:
                g = M("ro", h, l=l)
                o = g.open(pe)
                for j in range(4):
                    pe.wait_ge(sem("rsc_ready"), 16 * l + 4 * h + j + 1)
                    ins = pe.matmul(o[:, :], vv[:, j, h * P:(h + 1) * P], rsc[:, j, :], start=j == 0, stop=j == 3)
                g.close(ins)
            if h > 0:
                pe.wait_ge(sem("rsq_done"), 4 * l + h)
                g = M("rn", h - 1, l=l)
                o = g.open(pe)
                g.close(pe.matmul(o[:, :], C("ones"), rsq[:, :], start=True, stop=True))

    def ret_act(st, l):
        e = st.e
        for j in range(2):
            for t in range(2):
                m = 2 * j + t
                g = G("rg", j, t, l=l)
                o = g.take(e)
                if m == 0:
                    e.wait_ge(sem("rope_done"), 16 + 22 * l)
                st.w()
                st.f(e.activation(rg[:, m, :], o[:, :], ACT.Sigmoid), sem("rgs_ready"), 4 * l + m + 1)
            high(st, ("rg", j), G("rg", j, 1, l=l), l)
        def decays(h):
            e.wait_ge(sem("dexpo_ready"), 4 * l + h + 1)
            st.w()
            st.f(e.activation(dcy[:, h % 2, :], dcy[:, h % 2, :], ACT.Exp), sem("dcy_ready"), 4 * l + h + 1)

        decays(0)
        for h in range(5):
            if h < 3:
                decays(h + 1)
            if h > 0:
                e.wait_ge(sem("rc_ready"), 4 * l + h)
                st.w()
                st.f(e.activation(rsq[:, :], ro[:, (h - 1) % 2, :], ACT.Square), sem("rsq_done"), 4 * l + h)
            if h < 4:
                g = M("ro", h, l=l)
                o = g.take(e)
                if h >= 2:
                    e.wait_ge(sem("b_ready"), 27 + 20 * l + 4 + h - 1)
                st.w()
                g.done(st, e.activation(ro[:, h % 2, :], o[:, :], ACT.Copy))
                st.w()
                e.sem_inc(sem("ro_ready"), 1)
            if h > 0:
                g = M("rn", h - 1, l=l)
                o = g.take(e)
                st.w()
                g.done(st, e.activation(rsq[:, :], o[:, :], ACT.Sqrt, bias=C("eps")[:, 1:2], scale=1.0 / P))
                st.w()
                e.sem_inc(sem("rrt_ready"), 1)
                e.wait_ge(sem("rfin_ready"), 4 * l + h)
                st.f(e.activation(bH[:, h - 1, :], ro[:, (h - 1) % 2, :], ACT.Copy), sem("bH_ready"), 27 + 20 * l + 4 + h)

    def ret_dve(st, l):
        e = st.e
        for j in range(2):
            for t in range(2):
                m = 2 * j + t
                g = G("rg", j, t, l=l)
                o = g.take(e)
                e.wait_ge(sem("rgs_ready"), 4 * l + m + 1)
                st.w()
                g.done(st, e.tensor_tensor(rg[:, m, :], o[:, :], rg[:, m, :], ALU.mult))
            low(st, ("rg", j), l)
        e.wait_ge(sem("dst_in"), 16 * l + 16)

        def exponents(h):
            d = dcy[:, h % 2, :]
            st.w()
            st.s(e.tensor_scalar(d, dst[:, 0, :], lp[:, 26 + h:27 + h], None, ALU.mult))
            st.w()
            st.s(e.scalar_tensor_tensor(out=d, in0=dst[:, 1, :], scalar=lp[:, 30 + h:31 + h], in1=d,
                                        op0=ALU.mult, op1=ALU.add))
            st.w()
            e.sem_inc(sem("dexpo_ready"), 1)

        exponents(0)
        for h in range(5):
            if h < 3:
                exponents(h + 1)
            if h < 4:
                e.wait_ge(sem("dcy_ready"), 4 * l + h + 1)
                if h:
                    e.wait_ge(misc_ready, M("ro", h - 1, l=l).nth)
                for j in range(4):
                    g = G("rs", h, j, l=l)
                    o = g.take(e)
                    st.w()
                    g.done(st, e.scalar_tensor_tensor(out=rsc[:, j, :], in0=o[:, :], scalar=float(P) ** -0.5,
                                                      in1=dcy[:, h % 2, 3 * P - P * j:3 * P - P * j + S],
                                                      op0=ALU.mult, op1=ALU.mult))
                    st.w()
                    e.sem_inc(sem("rsc_ready"), 1)
            if h == 0:
                continue
            x = ro[:, (h - 1) % 2, :]
            g = M("rm", h - 1, l=l)
            o = g.take(e)
            st.w()
            g.done(st, e.scalar_tensor_tensor(out=x, in0=o[:, :], scalar=-1.0 / P, in1=x, op0=ALU.mult, op1=ALU.add))
            st.w()
            e.sem_inc(sem("rc_ready"), 1)
            e.wait_ge(sem("rrt_ready"), 4 * l + h)
            st.s(e.reciprocal(nrmt[:, :], nrmt[:, :]))
            st.w()
            st.s(e.scalar_tensor_tensor(out=x, in0=x, scalar=lp[:, 20 + h:21 + h], in1=nrmt[:, :], op0=ALU.mult, op1=ALU.mult))
            st.w()
            st.s(e.tensor_tensor(x, x, rg[:, h - 1, :], ALU.mult))
            st.w()
            e.sem_inc(sem("rfin_ready"), 1)
            e.wait_ge(sem("bH_ready"), 27 + 20 * l + 4 + h)
            st.s(e.tensor_tensor(bL[:, h - 1, :], x, bH[:, h - 1, :].bitcast(F32), ALU.subtract))
            st.w()
            e.sem_inc(sem("b_ready"), 1)

    msc = at("msc", [P, 2, S], F32, BASE + 49152)

    def mlp_sp(e, l):
        wu, wd = a["w_mlp_in_2"][l], a["w_mlp_out_2"][l]
        for r in range(2):
            with e.Fori(0, 4) as i:
                for j in range(2):
                    load(e, ("up", r, j), by_k(wu, KD, 2 * P, r * MR * P + i * 4 * P + j * 2 * P), l, i, 2)
            with e.Fori(0, 2) as i:
                for j in range(4):
                    load(e, ("dn", r, j), by_k(wd, MR, P, i * 4 * P + j * P, r * MR * P), l, i, 4)

    def mlp_pe(pe, l):
        for r in range(2):
            with pe.Fori(0, 4) as i:
                for j in range(2):
                    slot = use(pe, ("up", r, j), l, i, 2)
                    if r == 0 and j == 0:
                        product_pair(pe, [G("up", r, j, t, l=l, i=i, n=4) for t in range(2)], slot, KD, uH, uL,
                                     u_tile(1, l))
                        continue
                    for t in range(2):
                        g = G("up", r, j, t, l=l, i=i, n=4)
                        o = g.open(pe)
                        g.close(product(pe, o[:, :], slot, KD, 2 * P, t * P, P, uH, uL))
            with pe.Fori(0, 2) as i:
                for j in range(4):
                    slot = use(pe, ("dn", r, j), l, i, 4)
                    g = G("dn", r, j, l=l, i=i, n=4)
                    o = g.open(pe)
                    ready = lambda k: (sem("hid_ready"), 32 * l + MR * r + k + 1)
                    g.close(product(pe, o[:, :], slot, MR, P, 0, P, mH, mL, tile_ready=ready if j == 0 else None))

    mHf = mH[:, :, :].rearrange("p k s -> p (k s)")
    mLf = mL[:, :, :].rearrange("p k s -> p (k s)")

    def mlp_act(st, l):
        e = st.e
        for r in range(2):
            if r:
                e.wait_ge(gemm_ready, G("dn", 0, KD - 1, l=l).nth)

            def body(i):
                for j in range(2):
                    for t in range(2):
                        x = 32 * l + MR * r + 4 * i + 2 * j + t
                        g = G("up", r, j, t, l=l, i=i, n=4)
                        e.wait_ge(sem("sqr_ready"), x + 1)
                        st.w()
                        st.f(e.activation(mHf[:, ds((4 * i + 2 * j + t) * S, S)], msc[:, t, :], ACT.Copy), sem("hidH_ready"), x + 1)
                    high(st, ("up", r, j), g, l, i, 2)
            st.loop(4, 0, body)

            def body(i):
                for j in range(4):
                    high(st, ("dn", r, j), G("dn", r, j, l=l, i=i, n=4), l, i, 4)
            st.loop(2, 0, body)

    def mlp_dve(st, l):
        e = st.e
        for r in range(2):
            def body(i):
                for j in range(2):
                    for t in range(2):
                        x = 32 * l + MR * r + 4 * i + 2 * j + t
                        g = G("up", r, j, t, l=l, i=i, n=4)
                        o = g.take(e)
                        st.w()
                        st.s(e.tensor_scalar(msc[:, t, :], o[:, :], 0.0, None, ALU.max))
                        st.w()
                        g.done(st, e.tensor_tensor(msc[:, t, :], msc[:, t, :], msc[:, t, :], ALU.mult))
                        st.w()
                        e.sem_inc(sem("sqr_ready"), 1)
                        e.wait_ge(sem("hidH_ready"), x + 1)
                        dst = mLf[:, ds((4 * i + 2 * j + t) * S, S)]
                        hi = mHf[:, ds((4 * i + 2 * j + t) * S, S)]
                        st.f(e.tensor_tensor(dst, msc[:, t, :], hi.bitcast(F32), ALU.subtract), sem("hid_ready"), x + 1)
                    low(st, ("up", r, j), l, i, 2)
            st.loop(4, 4, body)

            def body(i):
                for j in range(4):
                    g = G("dn", r, j, l=l, i=i, n=4)
                    o = g.take(e)
                    tile = hTf[:, ds((4 * i + j) * S, S)]
                    st.w()
                    g.done(st, e.tensor_tensor(tile, tile, o[:, :], ALU.add))
                    if r == 1:
                        st.w()
                        e.sem_inc(sem("h_ready"), 1)
                    low(st, ("dn", r, j), l, i, 4)
            st.loop(2, 0, body)

    def layer_params(st, l):
        e = st.e
        for c, pack, col, n, step in ((0, 2, 88, 8, 8), (8, 2, 104, 8, 8), (16, 3, 0, 9, 9)):
            st.s(e.tensor_copy(lp[:, c:c + n], PTf[:, ds(pack * P + col + l * step, n)]))
        st.s(e.tensor_copy(lp[:, 25:34], layf[:, ds(l * 16, 9)]))
        st.w()

    PTf = PT[:, :, :].rearrange("p a b -> p (a b)")
    layf = lay[:, :, :].rearrange("p a b -> p (a b)")
    wb2 = a["w_branch_2"]
    outT = at("outT", [P, 2, D], F32, Z)

    block = nc.Block()
    with block:
        @block.sync
        def _(sp):
            setup_sp(sp)
            attn_sp(sp)
            gates = (w1, GATE0)
            merge_sp(sp, 0, a["w_a"][0], 3, gates)
            pool_sp(sp)
            merge_sp(sp, 1, a["w_b"][0], KD, gates)
            ssd_sp(sp)
            merge_sp(sp, 2, a["w_c"][0], KD, gates)
            out_sp(sp, a["w_o"][0])
            ffn_sp(sp)
            with sp.Fori(0, LAYERS) as l:
                gates = (w2[l], COL2["gate"])
                v_sp(sp, "dv", 2, l)
                rope_sp(sp, "d", l)
                merge_sp(sp, 0, wb2[l][0], 4, gates, l)
                v_sp(sp, "rv", 2, l)
                rope_sp(sp, "r", l)
                ret_sp(sp, l)
                merge_sp(sp, 1, wb2[l][1], 4, gates, l)
                v_sp(sp, "gv", 1, l)
                rope_sp(sp, "g", l)
                merge_sp(sp, 2, wb2[l][2], 4, gates, l)
                out_sp(sp, a["w_out_2"][l], l)
                mlp_sp(sp, l)
            for x in range(2):
                slot = (C2.k + x) % 2
                sp.wait_ge(lo_ready, C2.count + (C2.count - C2.base) + x - 1)
                for y in range(2):
                    sp.dma_start(wR[:, slot, y * D:(y + 1) * D], a["w_o"][0][y * P:(y + 1) * P, :]).then_inc(raw_ready[slot], 16)
            for t in range(NT):
                sp.wait_ge(sem("out_ready"), t + 1)
                sp.dma_start(out[0, t * P:(t + 1) * P, :], outT[:, t % 2, :]).then_inc(sem(f"out_done{t % 2}"), 16)
            for x in range(2):
                sp.wait_ge(sem(f"out_done{x}"), 16 * NT // 2)

        @block.gpsimd
        def _(pool):
            setup_pool(pool)
            attn_pool(pool)
            ssd_pool(pool)
            with pool.Fori(0, LAYERS) as l:
                rope_pool(pool, "d", l)
                rope_pool(pool, "r", l)
                ret_pool(pool, l)
                rope_pool(pool, "g", l)

        @block.tensor
        def _(pe):
            setup_pe(pe)
            norm_pe(pe, 0)
            attn_pe(pe)
            merge_pe(pe, 0, 3, 3)
            pool_pe(pe)
            merge_pe(pe, 1, KD, 11)
            ssd_pe(pe)
            merge_pe(pe, 2, KD, 19)
            out_pe(pe, 27)
            norm_pe(pe, 1)
            ffn_pe(pe)
            norm_pe(pe, 2)
            with pe.Fori(0, LAYERS) as l:
                norm_pe(pe, 0, l)
                v_pe(pe, "dv", 2, l)
                rope_pe(pe, "d", l)
                diff_pe(pe, l)
                merge_pe(pe, 0, 4, 27 + 20 * l + 4, l)
                v_pe(pe, "rv", 2, l)
                rope_pe(pe, "r", l)
                ret_pe(pe, l)
                merge_pe(pe, 1, 4, 27 + 20 * l + 8, l)
                v_pe(pe, "gv", 1, l)
                rope_pe(pe, "g", l)
                gqa_pe(pe, l)
                merge_pe(pe, 2, 4, 27 + 20 * l + 12, l)
                out_pe(pe, 27 + 20 * l + 20, l)
                norm_pe(pe, 1, l)
                mlp_pe(pe, l)
            pe.wait_ge(sem("h_ready"), 8 * (3 + 2 * LAYERS) + 8)
            for t in range(NT):
                for x in range(2):
                    n = 2 * t + x
                    if n >= 4:
                        pe.wait_ge(sem("out_taken"), n - 3)
                    for m in range(4):
                        ins = pe.transpose(ps[n % 4][:, m * P:(m + 1) * P], hT[:, 4 * x + m, t * P:(t + 1) * P], C("ident"))
                    ins.then_inc(sem("out_turned"), 1)

        @block.scalar
        def _(act):
            st = Steps(act, sem("act_step"))
            setup_act(st)
            act.wait_ge(sem("lines_out"), 48)
            norm_act(st, 0)
            attn_act(st)
            merge_act(st, 0)
            pool_act(st)
            merge_act(st, 1)
            ssd_act(st)
            merge_act(st, 2)
            split_act(st, lambda k: mg[:, k, :], 8, 19, lambda e, k: e.wait_ge(sem("sg_free"), 2 + 24))
            out_act(st)
            norm_act(st, 1)
            ffn_act(st)
            norm_act(st, 2)

            def layer(l):
                norm_act(st, 0, l)
                v_act(st, "dv", 2, l)
                rope_act(st, "d", l)
                diff_act(st, l)
                merge_act(st, 0, l)
                v_act(st, "rv", 2, l)
                rope_act(st, "r", l)
                ret_act(st, l)
                merge_act(st, 1, l)
                v_act(st, "gv", 1, l)
                rope_act(st, "g", l)
                gqa_act(st, l)
                merge_act(st, 2, l)
                split_act(st, lambda k: mg[:, k, :], 8, 27 + 20 * l + 12, lambda e, k: e.wait_ge(sem("sg_free"), 2 + 48 + 24 * l))
                out_act(st, l)
                norm_act(st, 1, l)
                mlp_act(st, l)
            st.loop(LAYERS, LAYER_STEPS["act"], layer)

        @block.vector
        def _(dve):
            st = Steps(dve, sem("dve_step"))
            setup_dve(st)
            norm_dve(st, 0, lambda k: PT[:, 0, k:k + 1])
            attn_dve(st)
            merge_dve(st, 0)
            pool_dve(st)
            merge_dve(st, 1)
            ssd_dve(st)
            merge_dve(st, 2)
            split_dve(st, lambda k: mg[:, k, :], 8, 19)
            out_dve(st)
            norm_dve(st, 1, lambda k: PT[:, 0, 108 + k:109 + k])
            ffn_dve(st)
            norm_dve(st, 2, lambda k: PT[:, 0, 116 + k:117 + k])

            def layer(l):
                layer_params(st, l)
                norm_dve(st, 0, lambda k: lp[:, k:k + 1], l)
                v_dve(st, "dv", 2, l)
                rope_dve(st, "d", l)
                diff_dve(st, l)
                merge_dve(st, 0, l)
                v_dve(st, "rv", 2, l)
                rope_dve(st, "r", l)
                ret_dve(st, l)
                merge_dve(st, 1, l)
                v_dve(st, "gv", 1, l)
                rope_dve(st, "g", l)
                gqa_dve(st, l)
                merge_dve(st, 2, l)
                split_dve(st, lambda k: mg[:, k, :], 8, 27 + 20 * l + 12)
                out_dve(st, l)
                norm_dve(st, 1, lambda k: lp[:, 8 + k:9 + k], l)
                mlp_dve(st, l)
            st.loop(LAYERS, LAYER_STEPS["dve"], layer)
            for t in range(NT):
                for x in range(2):
                    n = 2 * t + x
                    dve.wait_ge(sem("out_turned"), n + 1)
                    if x == 0 and t >= 2:
                        dve.wait_ge(sem(f"out_done{t % 2}"), 16 * (t // 2))
                    st.w()
                    st.f(dve.tensor_copy(outT[:, t % 2, x * S:(x + 1) * S], ps[n % 4][:, :]), sem("out_taken"), n + 1)
                st.w()
                dve.sem_inc(sem("out_ready"), 1)


LAYER_STEPS = dict(act=18, dve=406)


_INS = ["x", "rel_bias", "ln1_g", "w_in", "b_gate", "w_a", "pool_w", "pool_scale", "w_b", "ssd_conv_w", "ssd_conv_b",
        "ssd_dt_bias", "ssd_a_log", "ssd_d", "ssd_norm_w", "w_c", "w_o", "ln2_g", "ffn_w_up", "ffn_conv_w",
        "ffn_conv_b", "ffn_w_down", "final_g", "attn_norm_2", "w_in_2", "diff_q_norm_2", "diff_k_norm_2",
        "diff_lam_q1_2", "diff_lam_k1_2", "diff_lam_q2_2", "diff_lam_k2_2", "diff_subln_2", "ret_decay_fwd_2",
        "ret_decay_bwd_2", "ret_group_norm_2", "gqa_q_norm_2", "gqa_k_norm_2", "w_branch_2", "w_out_2",
        "mlp_norm_2", "w_mlp_in_2", "w_mlp_out_2"]


def kernel(**inputs):
    import concourse.bacc as _bacc
    from concourse.bass_utils import run_bass_kernel_spmd as _run

    nc = _bacc.Bacc("TRN2", target_bir_lowering=False, num_devices=1)
    arrays, args = {}, {}
    for name in _INS:
        x = np.ascontiguousarray(inputs[name])
        arrays[f"in_{name}_dram"] = x
        args[name] = nc.dram_tensor(f"in_{name}_dram", x.shape, mybir.dt.from_np(x.dtype), kind="ExternalInput").ap()
    tables = {}
    for name, x in (("consts", CONSTS), ("attn_consts", ATTN_CONSTS), ("ropes", rope_pack()), ("dists", dist_pack())):
        arrays[f"table_{name}_dram"] = x
        tables[name] = nc.dram_tensor(f"table_{name}_dram", x.shape, F32, kind="ExternalInput").ap()
    out = nc.dram_tensor("out_0_dram", (1, S, D), F32, kind="ExternalOutput").ap()
    lines = nc.dram_tensor("bias_lines_dram", (3 * HG, P, LINE), F32, kind="Internal").ap()
    build(nc, args, out, tables["consts"], tables["attn_consts"], tables["ropes"], tables["dists"], lines)
    r = _run(nc, [arrays], core_ids=[0])
    return r.results[0]["out_0_dram"]
```
